# Optimizing a Trainium2 kernel written in Bass

```python
import jax, jax.numpy as jnp
from jax import lax
import numpy as np
import math

D_MODEL = 1024
BATCH = 1
SEQ = 256
DEPTH = 2

MLA_HEADS = 16
MLA_Q_RANK = 384
MLA_KV_RANK = 256
MLA_NOPE = 64
MLA_ROPE = 32
MLA_QK = MLA_NOPE + MLA_ROPE
MLA_V = 64
ROPE_THETA = 10000.0
Q_BLOCK = 128
GLA_HEADS = 4
GLA_DK = D_MODEL // 2 // GLA_HEADS
GLA_DV = D_MODEL // GLA_HEADS
GLA_GATE_RANK = 16
GLA_TAU = 16.0
GLA_CHUNK = 64
PEER_HEADS = 8
PEER_NKEYS = 128
PEER_EXPERTS = PEER_NKEYS * PEER_NKEYS
PEER_QDIM = 128
PEER_HALF = PEER_QDIM // 2
PEER_TOPK = 16
PEER_BLOCK = 128
NORM_EPS = 1e-6
N_MLA = (DEPTH + 1) // 2
N_GLA = DEPTH // 2


def rms_norm(x, gain):
    xf = x.astype(jnp.float32)
    y = xf * lax.rsqrt(jnp.mean(xf * xf, axis=-1, keepdims=True) + NORM_EPS)
    return (y * gain.astype(jnp.float32)).astype(x.dtype)

def apply_rope(x, positions):
    half = x.shape[-1] // 2
    inv_freq = ROPE_THETA ** (-jnp.arange(half, dtype=jnp.float32) / half)
    ang = positions.astype(jnp.float32)[..., None] * inv_freq
    cos = jnp.cos(ang)[:, :, None, :]
    sin = jnp.sin(ang)[:, :, None, :]
    x1 = x[..., :half].astype(jnp.float32)
    x2 = x[..., half:].astype(jnp.float32)
    out = jnp.concatenate([x1 * cos - x2 * sin, x2 * cos + x1 * sin], axis=-1)
    return out.astype(x.dtype)

def causal_attention(q, k, v):
    B, S, H, Dqk = q.shape
    Dv = v.shape[-1]
    nb = S // Q_BLOCK
    scale = Dqk ** -0.5
    kh = k.transpose(0, 2, 1, 3)
    vh = v.transpose(0, 2, 1, 3)
    qb = q.reshape(B, nb, Q_BLOCK, H, Dqk).transpose(1, 0, 3, 2, 4)
    key_idx = jnp.arange(S)

    def one_block(args):
        qi, blk = args
        s = jnp.einsum('bhqd,bhkd->bhqk', qi, kh).astype(jnp.float32) * scale
        q_idx = blk * Q_BLOCK + jnp.arange(Q_BLOCK)
        mask = key_idx[None, :] <= q_idx[:, None]
        s = jnp.where(mask, s, -jnp.inf)
        p = jax.nn.softmax(s, axis=-1).astype(vh.dtype)
        return jnp.einsum('bhqk,bhkd->bhqd', p, vh)

    o = lax.map(one_block, (qb, jnp.arange(nb)))
    return o.transpose(1, 0, 3, 2, 4).reshape(B, S, H, Dv)

def mla_mixer(x, positions, w_down, g_q_lat, w_uq, g_kv_lat, w_ukv, g_qn, g_kn, w_o):
    B, S, _ = x.shape
    down = x @ w_down
    c_q = rms_norm(down[..., :MLA_Q_RANK], g_q_lat)
    c_kv = rms_norm(down[..., MLA_Q_RANK:MLA_Q_RANK + MLA_KV_RANK], g_kv_lat)
    k_rope = down[..., MLA_Q_RANK + MLA_KV_RANK:]
    q = (c_q @ w_uq).reshape(B, S, MLA_HEADS, MLA_QK)
    kv = (c_kv @ w_ukv).reshape(B, S, MLA_HEADS, MLA_NOPE + MLA_V)
    k = jnp.concatenate([kv[..., :MLA_NOPE],
                         jnp.broadcast_to(k_rope[:, :, None, :], (B, S, MLA_HEADS, MLA_ROPE))], axis=-1)
    v = kv[..., MLA_NOPE:]
    q = rms_norm(q, g_qn)
    k = rms_norm(k, g_kn)
    q = jnp.concatenate([q[..., :MLA_NOPE], apply_rope(q[..., MLA_NOPE:], positions)], axis=-1)
    k = jnp.concatenate([k[..., :MLA_NOPE], apply_rope(k[..., MLA_NOPE:], positions)], axis=-1)
    o = causal_attention(q, k, v)
    return o.reshape(B, S, MLA_HEADS * MLA_V) @ w_o

def chunked_gla(q, k, v, log_a):
    B, S, H, DK = q.shape
    DV = v.shape[-1]
    C = GLA_CHUNK
    n = S // C

    def to_chunks(t):
        return t.astype(jnp.float32).reshape(B, n, C, H, t.shape[-1]).transpose(1, 0, 3, 2, 4)

    qc, kc, vc, gc = to_chunks(q), to_chunks(k), to_chunks(v), to_chunks(log_a)
    b = jnp.cumsum(gc, axis=3)
    b_last = b[..., -1:, :]
    q_dec = qc * jnp.exp(b)
    k_inv = kc * jnp.exp(-b)
    causal = jnp.tril(jnp.ones((C, C), dtype=bool))
    attn = jnp.where(causal, jnp.einsum('nbhtk,nbhsk->nbhts', q_dec, k_inv), 0.0)
    o_intra = jnp.einsum('nbhts,nbhsv->nbhtv', attn, vc)
    kv_chunk = jnp.einsum('nbhsk,nbhsv->nbhkv', kc * jnp.exp(b_last - b), vc)
    chunk_decay = jnp.exp(b_last[..., 0, :])

    def step(state, inp):
        qd, kv, dec = inp
        o = jnp.einsum('bhtk,bhkv->bhtv', qd, state)
        return state * dec[..., None] + kv, o

    state0 = jnp.zeros((B, H, DK, DV), jnp.float32)
    _, o_inter = lax.scan(step, state0, (q_dec, kv_chunk, chunk_decay))
    o = o_intra + o_inter
    return o.transpose(1, 0, 3, 2, 4).reshape(B, S, H, DV)

def gla_mixer(x, w_in, w_g2, b_g, g_on, w_o):
    B, S, _ = x.shape
    HK = GLA_HEADS * GLA_DK
    HV = GLA_HEADS * GLA_DV
    proj = x @ w_in
    q = proj[..., :HK].reshape(B, S, GLA_HEADS, GLA_DK) * (GLA_DK ** -0.5)
    k = proj[..., HK:2 * HK].reshape(B, S, GLA_HEADS, GLA_DK)
    v = proj[..., 2 * HK:2 * HK + HV].reshape(B, S, GLA_HEADS, GLA_DV)
    r = proj[..., 2 * HK + HV:2 * HK + 2 * HV]
    g_low = proj[..., 2 * HK + 2 * HV:]
    log_a = jax.nn.log_sigmoid((g_low @ w_g2 + b_g).astype(jnp.float32)) / GLA_TAU
    log_a = log_a.reshape(B, S, GLA_HEADS, GLA_DK)
    o = chunked_gla(q, k, v, log_a)
    o = rms_norm(o, g_on).reshape(B, S, HV).astype(x.dtype)
    return (o * jax.nn.silu(r)) @ w_o

def peer_ffn(x, w_query, sub_keys, u_tab, v_tab):
    B, S, D = x.shape
    T = PEER_BLOCK
    nb = S // T
    xb = x.reshape(B, nb, T, D).transpose(1, 0, 2, 3)

    def one_block(xi):
        q = (xi @ w_query).reshape(B, T, PEER_HEADS, 2, PEER_HALF)
        s = jnp.einsum('bthcd,cnd->bthcn', q, sub_keys).astype(jnp.float32)
        s_top, i_top = lax.top_k(s, PEER_TOPK)
        cand = s_top[..., 0, :, None] + s_top[..., 1, None, :]
        cand_idx = i_top[..., 0, :, None] * PEER_NKEYS + i_top[..., 1, None, :]
        best, pos = lax.top_k(cand.reshape(B, T, PEER_HEADS, PEER_TOPK * PEER_TOPK), PEER_TOPK)
        idx = jnp.take_along_axis(cand_idx.reshape(B, T, PEER_HEADS, PEER_TOPK * PEER_TOPK), pos, axis=-1)
        gate = jax.nn.softmax(best, axis=-1)
        u = u_tab[idx]
        h = jax.nn.gelu(jnp.einsum('bthkd,btd->bthk', u, xi).astype(jnp.float32), approximate=False)
        w = (gate * h).astype(xi.dtype)
        return jnp.einsum('bthk,bthkd->btd', w, v_tab[idx])

    out = lax.map(one_block, xb)
    return out.transpose(1, 0, 2, 3).reshape(B, S, D)

def first_inputs(seed: int = 0) -> dict:
    key = jax.random.key(seed)
    ks = jax.random.split(key, 24)

    def normal(k, shape, scale):
        return jax.random.normal(k, shape, jnp.float32) * scale

    def gain(k, shape):
        return 1.0 + 0.02 * jax.random.normal(k, shape, jnp.float32)

    D = D_MODEL
    HK = GLA_HEADS * GLA_DK
    HV = GLA_HEADS * GLA_DV
    x = jax.random.normal(ks[0], (BATCH, SEQ, D), jnp.float32)
    offsets = jax.random.randint(ks[1], (BATCH, 1), 0, 4096, dtype=jnp.int32)
    positions = (offsets + jnp.arange(SEQ, dtype=jnp.int32)[None, :]).astype(jnp.int32)
    return {
        "x": x,
        "positions": positions,
        "attn_norm_g": gain(ks[2], (DEPTH, D)),
        "ffn_norm_g": gain(ks[3], (DEPTH, D)),
        "mla_w_down": normal(ks[4], (N_MLA, D, MLA_Q_RANK + MLA_KV_RANK + MLA_ROPE), D ** -0.5),
        "mla_g_q_lat": gain(ks[5], (N_MLA, MLA_Q_RANK)),
        "mla_w_uq": normal(ks[6], (N_MLA, MLA_Q_RANK, MLA_HEADS * MLA_QK), MLA_Q_RANK ** -0.5),
        "mla_g_kv_lat": gain(ks[7], (N_MLA, MLA_KV_RANK)),
        "mla_w_ukv": normal(ks[8], (N_MLA, MLA_KV_RANK, MLA_HEADS * (MLA_NOPE + MLA_V)), MLA_KV_RANK ** -0.5),
        "mla_g_qn": gain(ks[9], (N_MLA, MLA_QK)),
        "mla_g_kn": gain(ks[10], (N_MLA, MLA_QK)),
        "mla_w_o": normal(ks[11], (N_MLA, MLA_HEADS * MLA_V, D), (MLA_HEADS * MLA_V) ** -0.5),
        "gla_w_in": normal(ks[12], (N_GLA, D, 2 * HK + 2 * HV + GLA_GATE_RANK), D ** -0.5),
        "gla_w_g2": normal(ks[13], (N_GLA, GLA_GATE_RANK, HK), GLA_GATE_RANK ** -0.5),
        "gla_b_g": normal(ks[14], (N_GLA, HK), 0.02),
        "gla_g_on": gain(ks[15], (N_GLA, GLA_DV)),
        "gla_w_o": normal(ks[16], (N_GLA, HV, D), HV ** -0.5),
        "peer_w_query": normal(ks[17], (DEPTH, D, PEER_HEADS * PEER_QDIM), D ** -0.5),
        "peer_sub_keys": normal(ks[18], (DEPTH, 2, PEER_NKEYS, PEER_HALF), PEER_HALF ** -0.5),
        "peer_u": normal(ks[19], (DEPTH, PEER_EXPERTS, D), D ** -0.5),
        "peer_v": normal(ks[20], (DEPTH, PEER_EXPERTS, D), 0.5 * PEER_HEADS ** -0.5),
    }

def first_block(x, positions, attn_norm_g, ffn_norm_g, mla_w_down, mla_g_q_lat, mla_w_uq, mla_g_kv_lat,
              mla_w_ukv, mla_g_qn, mla_g_kn, mla_w_o, gla_w_in, gla_w_g2, gla_b_g, gla_g_on, gla_w_o,
              peer_w_query, peer_sub_keys, peer_u, peer_v):
    h = x
    for i in range(DEPTH):
        hn = rms_norm(h, attn_norm_g[i])
        j = i // 2
        if i % 2 == 0:
            mix = mla_mixer(hn, positions, mla_w_down[j], mla_g_q_lat[j], mla_w_uq[j], mla_g_kv_lat[j],
                            mla_w_ukv[j], mla_g_qn[j], mla_g_kn[j], mla_w_o[j])
        else:
            mix = gla_mixer(hn, gla_w_in[j], gla_w_g2[j], gla_b_g[j], gla_g_on[j], gla_w_o[j])
        h = h + mix
        h = h + peer_ffn(rms_norm(h, ffn_norm_g[i]), peer_w_query[i], peer_sub_keys[i], peer_u[i], peer_v[i])
    return h


DEPTH_2 = 1

CHUNK = 64
D_CONV = 1024
CONV_WIDTH = 3
HEAD_DIM = 64
N_HEADS = 16
D_ATT = N_HEADS * HEAD_DIM
N_GROUPS = 4
EXPERTS_PER_GROUP = 8
N_EXPERTS = N_GROUPS * EXPERTS_PER_GROUP
TOP_K = 2
D_EXPERT = 512
MOE_BLOCK = 256
EPS = 1e-6

SPLITS = (D_CONV, D_CONV, D_CONV, D_ATT, D_ATT, D_ATT, N_HEADS, D_MODEL, D_MODEL)
D_IN_PROJ = sum(SPLITS)


def rmsnorm(x, g):
    xf = x.astype(jnp.float32)
    y = xf * lax.rsqrt(jnp.mean(xf * xf, axis=-1, keepdims=True) + EPS)
    return (y * g.astype(jnp.float32)).astype(x.dtype)

def split_cols(p):
    idx = np.cumsum(np.array(SPLITS))[:-1].tolist()
    return jnp.split(p, idx, axis=-1)

def short_conv(b, c, u, conv_w, conv_b):
    S = u.shape[1]
    z = c * u
    zp = jnp.pad(z, ((0, 0), (CONV_WIDTH - 1, 0), (0, 0)))
    acc = conv_b
    for i in range(CONV_WIDTH):
        acc = acc + conv_w[i] * zp[:, i:i + S]
    return b * acc

def forgetting_attention(q, k, v, f_logit, b_forget):
    B, S, H, dh = q.shape
    log_f = jax.nn.log_sigmoid(f_logit.astype(jnp.float32) + b_forget.astype(jnp.float32))
    cum = jnp.transpose(jnp.cumsum(log_f, axis=1), (0, 2, 1))
    scale = 1.0 / math.sqrt(dh)
    outs = []
    for qb in range(S // Q_BLOCK):
        qs, qe = qb * Q_BLOCK, (qb + 1) * Q_BLOCK
        qblk = q[:, qs:qe]
        kp, vp = k[:, :qe], v[:, :qe]
        s = jnp.einsum('bqhd,bkhd->bhqk', qblk, kp).astype(jnp.float32) * scale
        s = s + (cum[:, :, qs:qe, None] - cum[:, :, None, :qe])
        t_pos = jnp.arange(qs, qe)[:, None]
        s_pos = jnp.arange(qe)[None, :]
        s = jnp.where(s_pos <= t_pos, s, -jnp.inf)
        p = jax.nn.softmax(s, axis=-1).astype(v.dtype)
        outs.append(jnp.einsum('bhqk,bkhd->bqhd', p, vp))
    return jnp.concatenate(outs, axis=1)

def token_mixer(h, w_in, conv_w, conv_b, b_forget, w_conv_out, w_att_out, w_out):
    B, S, _ = h.shape
    proj = h @ w_in
    cb, cc, cu, q, k, v, f_logit, g_conv, g_att = split_cols(proj)
    y_conv = short_conv(cb, cc, cu, conv_w, conv_b) @ w_conv_out
    o = forgetting_attention(q.reshape(B, S, N_HEADS, HEAD_DIM),
                             k.reshape(B, S, N_HEADS, HEAD_DIM),
                             v.reshape(B, S, N_HEADS, HEAD_DIM),
                             f_logit, b_forget)
    y_att = o.reshape(B, S, D_ATT) @ w_att_out
    m = jax.nn.sigmoid(g_conv) * y_conv + jax.nn.sigmoid(g_att) * y_att
    return m @ w_out

def hier_moe(h, w_router_group, w_router_expert, w_e_gate, w_e_up, w_e_down):
    B, S, D = h.shape
    T = B * S
    hf = h.reshape(T, D)
    pg = jax.nn.softmax((hf @ w_router_group).astype(jnp.float32), axis=-1)
    g_val, g_idx = lax.top_k(pg, 1)
    le = jnp.einsum('td,gde->tge', hf, w_router_expert).astype(jnp.float32)
    le_sel = jnp.take_along_axis(le, g_idx[:, :, None], axis=1)[:, 0]
    pe = jax.nn.softmax(le_sel, axis=-1)
    e_val, e_idx = lax.top_k(pe, TOP_K)
    e_val = e_val / jnp.sum(e_val, axis=-1, keepdims=True)
    w_tok = (g_val * e_val).astype(h.dtype)
    expert = (g_idx * EXPERTS_PER_GROUP + e_idx).astype(jnp.int32)

    A = T * TOP_K
    flat_e = expert.reshape(A)
    flat_w = w_tok.reshape(A)
    flat_tok = jnp.arange(A, dtype=jnp.int32) // TOP_K
    order = jnp.argsort(flat_e)
    sorted_e = flat_e[order]
    counts = jnp.bincount(flat_e, length=N_EXPERTS)
    padded = (counts + MOE_BLOCK - 1) // MOE_BLOCK * MOE_BLOCK
    start_sorted = jnp.cumsum(counts) - counts
    end_padded = jnp.cumsum(padded)
    start_padded = end_padded - padded
    rank = jnp.arange(A, dtype=jnp.int32) - start_sorted[sorted_e]
    dest = start_padded[sorted_e] + rank
    n_rows = A + N_EXPERTS * MOE_BLOCK
    n_blocks = n_rows // MOE_BLOCK
    row_tok = jnp.zeros((n_rows,), jnp.int32).at[dest].set(flat_tok[order])
    row_w = jnp.zeros((n_rows,), h.dtype).at[dest].set(flat_w[order])
    block_e = jnp.minimum(
        jnp.searchsorted(end_padded, jnp.arange(n_blocks) * MOE_BLOCK, side='right'),
        N_EXPERTS - 1).astype(jnp.int32)
    x_rows = hf[row_tok].reshape(n_blocks, MOE_BLOCK, D)

    def expert_block(args):
        xb, e = args
        a = xb @ w_e_gate[e]
        u = xb @ w_e_up[e]
        return (jax.nn.silu(a) * u) @ w_e_down[e]

    y_rows = lax.map(expert_block, (x_rows, block_e)).reshape(n_rows, D)
    y = jax.ops.segment_sum(y_rows * row_w[:, None], row_tok, num_segments=T)
    return y.reshape(B, S, D)

def second_inputs(seed: int = 0) -> dict:
    key = jax.random.key(seed)
    ks = jax.random.split(key, 20)
    f32 = jnp.float32
    nrm = lambda k, shape, fan: jax.random.normal(k, shape, f32) * (fan ** -0.5)
    return {
        "x": jax.random.normal(ks[0], (BATCH, SEQ, D_MODEL), f32),
        "norm_mix_g": 1.0 + 0.02 * jax.random.normal(ks[1], (D_MODEL,), f32),
        "w_in": nrm(ks[2], (D_MODEL, D_IN_PROJ), D_MODEL),
        "conv_w": nrm(ks[3], (CONV_WIDTH, D_CONV), CONV_WIDTH),
        "conv_b": 0.01 * jax.random.normal(ks[4], (D_CONV,), f32),
        "b_forget": jax.random.uniform(ks[5], (N_HEADS,), f32, 1.0, 6.0),
        "w_conv_out": nrm(ks[6], (D_CONV, D_MODEL), D_CONV),
        "w_att_out": nrm(ks[7], (D_ATT, D_MODEL), D_ATT),
        "w_out": nrm(ks[8], (D_MODEL, D_MODEL), D_MODEL),
        "norm_ffn_g": 1.0 + 0.02 * jax.random.normal(ks[9], (D_MODEL,), f32),
        "w_router_group": nrm(ks[10], (D_MODEL, N_GROUPS), D_MODEL),
        "w_router_expert": nrm(ks[11], (N_GROUPS, D_MODEL, EXPERTS_PER_GROUP), D_MODEL),
        "w_e_gate": nrm(ks[12], (N_EXPERTS, D_MODEL, D_EXPERT), D_MODEL),
        "w_e_up": nrm(ks[13], (N_EXPERTS, D_MODEL, D_EXPERT), D_MODEL),
        "w_e_down": nrm(ks[14], (N_EXPERTS, D_EXPERT, D_MODEL), D_EXPERT),
        "norm_final_g": 1.0 + 0.02 * jax.random.normal(ks[15], (D_MODEL,), f32),
    }

def second_block(x, norm_mix_g, w_in, conv_w, conv_b, b_forget, w_conv_out, w_att_out, w_out,
              norm_ffn_g, w_router_group, w_router_expert, w_e_gate, w_e_up, w_e_down,
              norm_final_g):
    for _ in range(DEPTH_2):
        x = x + token_mixer(rmsnorm(x, norm_mix_g), w_in, conv_w, conv_b, b_forget,
                            w_conv_out, w_att_out, w_out)
        x = x + hier_moe(rmsnorm(x, norm_ffn_g), w_router_group, w_router_expert,
                         w_e_gate, w_e_up, w_e_down)
    return rmsnorm(x, norm_final_g)


def setup_inputs(seed=0):
    out = dict(first_inputs(seed))
    for name, value in second_inputs(seed + 1).items():
        if name != "x":
            out[name + "_2"] = value
    return out


def reference(
    x, positions, attn_norm_g, ffn_norm_g, mla_w_down, mla_g_q_lat, mla_w_uq, mla_g_kv_lat,
    mla_w_ukv, mla_g_qn, mla_g_kn, mla_w_o, gla_w_in, gla_w_g2, gla_b_g, gla_g_on, gla_w_o,
    peer_w_query, peer_sub_keys, peer_u, peer_v, norm_mix_g_2, w_in_2, conv_w_2, conv_b_2,
    b_forget_2, w_conv_out_2, w_att_out_2, w_out_2, norm_ffn_g_2, w_router_group_2,
    w_router_expert_2, w_e_gate_2, w_e_up_2, w_e_down_2, norm_final_g_2,
):
    x = first_block(
        x, positions, attn_norm_g, ffn_norm_g, mla_w_down, mla_g_q_lat, mla_w_uq, mla_g_kv_lat,
        mla_w_ukv, mla_g_qn, mla_g_kn, mla_w_o, gla_w_in, gla_w_g2, gla_b_g, gla_g_on, gla_w_o,
        peer_w_query, peer_sub_keys, peer_u, peer_v,
    )
    return second_block(
        x, norm_mix_g_2, w_in_2, conv_w_2, conv_b_2, b_forget_2, w_conv_out_2, w_att_out_2,
        w_out_2, norm_ffn_g_2, w_router_group_2, w_router_expert_2, w_e_gate_2, w_e_up_2,
        w_e_down_2, norm_final_g_2,
    )


_drawn_inputs = setup_inputs


def setup_inputs(seed=0):
    import zlib

    import numpy as np

    out = dict(_drawn_inputs(seed))
    spreads = {}
    factors = {'gla_b_g': 3.02, 'conv_b_2': 4.092, 'norm_final_g_2': 2.881}
    for name, (base, spread) in spreads.items():
        noise = np.random.default_rng([zlib.crc32(name.encode()), seed]).standard_normal(out[name].shape)
        drawn = base * np.exp(spread * noise) if base else spread * noise
        out[name] = __import__('jax').numpy.asarray(drawn.astype(out[name].dtype))
    for name, factor in factors.items():
        out[name] = (out[name] * factor).astype(out[name].dtype)
    return out
```

```python
import numpy as np
import concourse.bass as bass
from concourse import mybir
from contextlib import ExitStack

P = 128
S, D = 256, 1024
NT = S // P
KD = D // P
BANK = 512
EPS = 1e-6
NEG = -1e30

QR, KVR, ROPE, NOPE, DV = 384, 256, 32, 64, 64
H, QK = 16, NOPE + ROPE
HALF = ROPE // 2
GH, GDK, GDV, GR, CH = 4, 128, 256, 16, 64
TAU = 16.0
PH, PK, NKEYS = 8, 16, 128
NEXP = NKEYS * NKEYS
FH, FD = 16, 64
NG, EPG, NE, F = 4, 8, 32, 512
SLOTS = 64
ROUNDS = S // SLOTS
PAIRS = NE // 2

NW = 4
RU, RV = 4, 4
NB = 6

BEFORE = [("mla", 0), ("route", 0)]
BESIDE = [[("mla", 1), ("route", 1)], [("gla", 0), ("route", 2)], [("gla", 1), ("route", 3)], []]
AFTER = [("mix", 0), ("moe", 0)]
STAGES = BEFORE + [key for beside in BESIDE for key in beside] + AFTER
QUART = 4
QUARTERS = (PH + 1) * PK // QUART


def attention_jobs(t):
    jobs = [f"S{t}_0", f"S{t}_1"]
    for g in range(H // 2):
        jobs.append(f"T{t}_{g}")
        if g + 2 < H // 2:
            jobs.append(f"S{t}_{g + 2}")
        jobs.append(f"O{t}_{g}")
    return jobs


def stage_jobs(stage, v):
    if stage == "mla":
        return (["x0", "x1", "down0", "down1", "cq", "ckv", "q0", "q1", "q2", "kv0", "kv1", "kv2", "kv3"]
                + [f"qT{i}" for i in range(4)] + [f"kT{i}" for i in range(4)] + attention_jobs(v) + ["out0", "out1"])
    if stage == "route":
        return ["x0", "x1", "q0", "q1"] + [f"s{i}" for i in range(4)]
    if stage == "gla":
        return ["x0", "x1", "q", "k", "v0", "v1", "r0", "r1", "low", "gate", "kd", "at", "kv00", "kv01", "kv10",
                "kv11", "o0", "o1", "oT0", "oT1", "out0", "out1"]
    if stage == "mix":
        return (["x00", "x01", "x10", "x11"]
                + [f"{m}{i}" for m in ("cc", "cu", "cb", "q", "k") for i in range(4)]
                + ["v00", "v01", "v10", "v11", "f"] + [f"{m}{i}" for m in ("gc", "ga") for i in range(4)]
                + attention_jobs(0) + attention_jobs(1)
                + [f"yc{i}" for i in range(4)] + [f"ya{i}" for i in range(4)] + ["o00", "o01", "o10", "o11"])
    return ["x00", "x01", "x10", "x11", "r0", "r1", "rank"]


def attention_steps(t, kind):
    names = {"dve": ("m", "p"), "act": ("e",)}[kind]
    return [f"{n}{t}_{g}" for g in range(H // 2) for n in names]


def stage_steps(kind, stage, v):
    if kind == "dve":
        if stage == "mla":
            return (["xn", "cos_arg", "lat", "qk"] + attention_order(v) + ["resid"])
        if stage == "route":
            return ["xn", "shift", "ready"]
        if stage == "gla":
            return ["xn", "abs", "b", "qd", "kd", "at", "state1", "on", "state2", "resid"]
        if stage == "mix":
            return (["xn0", "xn1", "abs", "cum"] + attention_order(0) + attention_order(1)
                    + ["convy", "m", "resid"])
        return ["xn0", "xn1", "gshift", "eshift", "picked", "keys"]
    if stage == "mla":
        return ["trig"] + [f"e{v}_{g}" for g in range(H // 2)]
    if stage == "route":
        return ["exp"]
    if stage == "gla":
        return ["exp", "ln", "eb", "ekd"]
    if stage == "mix":
        return ["exp", "ln"] + [f"e{t}_{g}" for t in range(2) for g in range(H // 2)]
    return ["gexp", "eexp"]


def attention_order(t):
    out = [f"m{t}_0"]
    for g in range(H // 2):
        if g + 1 < H // 2:
            out.append(f"m{t}_{g + 1}")
        out.append(f"p{t}_{g}")
    return out


def number(lists):
    out, n = {}, 0
    for key in STAGES:
        for name in lists(*key):
            n += 1
            out[key + (name,)] = n
    return out


JOB = number(stage_jobs)
STEP = {kind: number(lambda s, v, kind=kind: stage_steps(kind, s, v)) for kind in ("dve", "act")}


def stage_quarters(stage, v):
    if (stage, v) in BEFORE + AFTER:
        return {}
    if stage == "mla":
        return {"x1": 1, "down0": 1, "down1": 1, "cq": 1, "q1": 1, "kv0": 1, "kv3": 3, "kT3": 1,
                **{f"O{v}_{g}": 1 for g in range(H // 2)}, "out0": 1}
    if stage == "route":
        return {"x1": 1, "q0": 1, "q1": 1, "s3": 10}
    return {"x1": 1, "q": 1, "k": 1, "v0": 1, "v1": 1, "r0": 1, "r1": 1, "gate": 3, "kd": 1, "at": 1,
            "kv11": 1, "o1": 2, "oT1": 1, "out0": 1}


def quarter_marks():
    out = []
    for beside in BESIDE:
        marks = []
        for key in beside:
            for name, n in stage_quarters(*key).items():
                marks += [JOB[key + (name,)]] * n
        out.append(sorted(marks)[:QUARTERS])
    return out


QUARTER_MARKS = quarter_marks()


class Quarters:

    def __init__(self, take):
        self.take, self.g, self.n = take, None, 0

    def open(self, g):
        self.g, self.n = g, 0

    def upto(self, job):
        while self.g is not None and self.n < len(QUARTER_MARKS[self.g]) and QUARTER_MARKS[self.g][self.n] <= job:
            self.one()

    def one(self):
        self.take(self.g, self.n // (PK // QUART), self.n % (PK // QUART))
        self.n += 1

    def tick(self, job):
        if self.g is not None and self.n < len(QUARTER_MARKS[self.g]) and QUARTER_MARKS[self.g][self.n] <= job:
            self.one()

    def close(self):
        while self.n < QUARTERS:
            self.one()
        self.g = None


def stage_pieces(stage, v):
    def two(w, names, c0=0):
        return [(w, c0, BANK, names[0]), (w, c0 + BANK, BANK, names[1])]
    if stage == "mla":
        return ([("attn_gain0", 0, D, "x1"), ("w_down", 0, BANK, "down0"), ("w_down", BANK, QR + KVR + ROPE - BANK, "down1")]
                + [("w_uq", i * BANK, BANK, f"q{i}") for i in range(3)]
                + [("w_ukv", i * BANK, BANK, f"kv{i}") for i in range(4)]
                + two("mla_w_o", ["out0", "out1"]))
    if stage == "route":
        return [(f"ffn_gain{v // 2}", 0, D, "x1")] + two(f"w_query{v // 2}", ["q0", "q1"])
    if stage == "gla":
        return ([("attn_gain1", 0, D, "x1"), ("gla_w_in", 0, BANK, "q"), ("gla_w_in", BANK, BANK, "k")]
                + two("gla_w_in", ["v0", "v1"], 2 * BANK) + two("gla_w_in", ["r0", "r1"], 4 * BANK)
                + [("gla_w_in", 6 * BANK, GR, "low")] + two("gla_w_o", ["out0", "out1"]))
    if stage == "mix":
        out = [("mix_gain", 0, D, "x11")]
        for m, c in (("cc", 1), ("cu", 2), ("cb", 0), ("q", 3), ("k", 4)):
            out += two("w_in_2", [f"{m}1", f"{m}3"], c * D)
        out += two("w_in_2", ["v01", "v11"], 5 * D) + [("w_in_2", 6 * D, FH, "f")]
        for m, c in (("gc", 6), ("ga", 7)):
            out += two("w_in_2", [f"{m}1", f"{m}3"], c * D + FH)
        return out + two("w_conv_out", ["yc1", "yc3"]) + two("w_att_out", ["ya1", "ya3"]) + two("w_out", ["o01", "o11"])
    return [("moe_gain", 0, D, "x11"), ("w_router", 0, NG + NE, "r1")]


PIECES = [(key, piece) for key in STAGES for piece in stage_pieces(*key)]


def build(nc, a, out):
    f32, i32, u32 = mybir.dt.float32, mybir.dt.int32, mybir.dt.uint32
    ALU, ACT, AX = mybir.AluOpType, mybir.ActivationFunctionType, mybir.AxisListType
    X = AX.X
    ctx = ExitStack()
    with ctx:
        def sb(name, shape, dt=f32):
            return ctx.enter_context(nc.sbuf_tensor(name, shape, dt))

        def sem(name):
            return ctx.enter_context(nc.semaphore(name))

        h = sb("h", [P, NT, D])
        ident = sb("ident", [P, P])
        causal = sb("causal", [P, P])
        ones = sb("ones", [P, P])
        zeros = sb("zeros", [P, P])
        before = sb("before", [P, P])
        chunk_causal = sb("chunk_causal", [P, CH])
        iota16 = sb("iota16", [P, PK])
        iota64 = sb("iota64", [P, SLOTS])
        inv_freq = sb("inv_freq", [P, HALF])
        pos_i = sb("pos_i", [P, NT], i32)
        lat_gain = sb("lat_gain", [P, QR + KVR])
        qn_gain = sb("qn_gain", [P, QK])
        kn_gain = sb("kn_gain", [P, QK])
        on_gain = sb("on_gain", [P, GDV])
        b_gate = sb("b_gate", [P, GH])
        w_g2 = sb("w_g2", [GR, GH * GDK])
        sub_keys = sb("sub_keys", [P, 2, NKEYS])
        conv_w = sb("conv_w", [P, 3, KD])
        conv_b = sb("conv_b", [P, KD])
        b_forget = sb("b_forget", [FH, 1])
        small = sb("small", [P, 256])

        ring = sb("ring", [P, NW, KD * BANK])
        rows = sb("rows", [P, (RU + RV) * D])
        u_rows = rows[:, 0:RU * D].rearrange("p (r d) -> p r d", r=RU)
        v_rows = rows[:, RU * D:(RU + RV) * D].rearrange("p (r d) -> p r d", r=RV)

        kept = sb("kept", [P, 6144])
        work = sb("work", [P, 12304])
        px = sb("px", [P, 2, D])
        idx = sb("idx", [P, 2, P], i32)
        gate = sb("gate", [P, 2, P])
        hid = sb("hid", [P, P])
        gel = sb("gel", [P, P])
        wgt = sb("wgt", [P, P])
        diag = sb("diag", [P, 4, P])
        junk = sb("junk", [P, D])
        list_u = sb("list_u", [P, 2, PK], i32)
        list_v = sb("list_v", [P, 2, PK], i32)

        psum = ctx.enter_context(nc.psum_tensor("psum", [P, 8, BANK], f32))

        def carve(region, at, *shape):
            n = int(np.prod(shape))
            v = region[:, at:at + n]
            if len(shape) == 2:
                v = v.rearrange("p (a b) -> p a b", a=shape[0])
            if len(shape) == 3:
                v = v.rearrange("p (a b c) -> p a b c", a=shape[0], b=shape[1])
            return v

        xn = carve(work, 0, D)
        xT = carve(work, 1024, KD, P)
        m_lat, m_cT = carve(work, 2048, QR + KVR + ROPE), carve(work, 2720, 5, P)
        m_q, m_k = carve(work, 3360, H, QK), carve(work, 4896, H, QK)
        m_qT = carve(work, 6432, H, P)
        m_oT = carve(work, 8480, H // 2, P)
        m_sq = carve(work, 9504, H, QK)
        m_S = carve(work, 9504, 2, BANK)
        m_pT = carve(work, 10528, 2, BANK)
        m_rope = carve(work, 1024, 4, H, HALF)
        m_trig = carve(work, 11552, 4, HALF)
        k_T = carve(kept, 0, H, S)
        k_V = carve(kept, 4096, NT, D)

        r_S = carve(work, 2048, 2 * PH, NKEYS)
        r_c = carve(work, 4096, PH, PK * PK)
        r_t = carve(work, 6144, PH, PK * PK)
        r_qT = carve(work, 8192, PH, P)
        r_val = carve(work, 9216, 2 * PH, PK)
        r_idx = carve(work, 9472, 2 * PH, PK)
        r_idf = carve(work, 9728, 2 * PH, PK)
        r_best = carve(work, 9984, PH, PK)
        r_pos = carve(work, 10112, PH, PK)
        r_ab = carve(work, 10240, 2, P)
        r_sel = carve(work, 10496, 2, P)

        g_qT, g_kT = carve(work, 2048, GH, P), carve(work, 2560, GH, P)
        g_v, g_r = carve(work, 3072, D), carve(work, 4096, D)
        g_low, g_z = carve(work, 5120, P), carve(work, 5248, GH, P)
        g_e, g_b = carve(work, 5760, GH, P), carve(work, 6272, GH, P)
        g_eb, g_enb = carve(work, 6784, GH, P), carve(work, 7296, GH, P)
        g_kd, g_kdn = carve(work, 7808, GH, P), carve(work, 8320, GH, P)
        g_at = carve(work, 8832, GH, CH)
        g_kv = carve(work, 9088, 2, D)
        g_o = carve(work, 11136, D)
        g_mid = carve(kept, 0, GH, GDV)
        g_state = carve(kept, 1024, GH, GDV)

        x_xT = carve(work, 0, KD, S)
        x_z = carve(work, 2048, KD, S + 2)
        x_q, x_k = carve(work, 4112, KD, S), carve(work, 6160, KD, S)
        x_v = carve(work, 8208, NT, D)
        x_oT = carve(work, 10256, KD, S)
        x_cum, x_f = diag[:, 2:4, :].rearrange("p a b -> p (a b)"), carve(kept, 3072, S)
        x_cc, x_cb = carve(rows, 0, KD, S), carve(rows, 2048, KD, S)
        x_gc, x_ga = carve(rows, 4096, KD, S), carve(rows, 6144, KD, S)
        x_S, x_pT = (px[:, i, :].rearrange("p (a b) -> p a b", a=2) for i in range(2))
        x_ncum = diag[:, 0:2, :].rearrange("p a b -> p (a b)")
        x_xn = carve(kept, 2048, D)
        x_yc, x_ya = x_cc, carve(kept, 0, KD, S)

        hn = carve(work, 0, NT, D)
        e_xT = carve(work, 2048, KD, P)
        e_X = carve(work, 3072, 2, D)
        e_P = carve(work, 5120, NT, P)
        e_Pw = carve(work, 5376, NT, P)
        e_PwT = carve(work, 5632, NT, P)
        e_silu = carve(work, 11520, 2, 4 * SLOTS)
        e_act = carve(work, 6144, 2, 4, SLOTS)
        e_y = carve(work, 6656, D)
        e_lg = carve(work, 7680, NT, NG + NE)
        e_pg = carve(work, 7760, NT, 8)
        e_pe = carve(work, 7776, NT, EPG)
        e_oh = carve(work, 7792, NT, 8)
        e_A, e_W = carve(work, 7808, NT, NE), carve(work, 7872, NT, NE)
        e_rank = carve(work, 7936, 3, NE)
        e_key = carve(work, 8032, ROUNDS, NT * NE)
        e_top = carve(work, 8288, 2, 8)
        e_tmp = carve(work, 8304, 4, NE)
        e_cnt = sb("e_cnt", [P, 2])
        e_cnt_i = sb("e_cnt_i", [P, 2], i32)
        e_out = carve(work, 8448, NT, D)
        fin_gain = carve(work, 10496, D)

        const_ready = sem("const_ready")
        loaded = sem("loaded")
        weights = [sem(f"weights{i}") for i in range(NW)]
        filled = sem("filled")
        emptied = sem("emptied")
        dve_step = sem("dve_step")
        act_step = sem("act_step")
        dve_link = sem("dve_link")
        act_link = sem("act_link")
        u_here = [sem(f"u_here{i}") for i in range(RU)]
        v_here = [sem(f"v_here{i}") for i in range(RV)]
        u_used = sem("u_used")
        v_used = sem("v_used")
        granted = sem("granted")
        listed = sem("listed")
        gelu_ready = sem("gelu_ready")
        wgt_ready = sem("wgt_ready")
        diag_ready = sem("diag_ready")
        experts_added = sem("experts_added")
        e_w = [sem(f"e_w{i}") for i in range(6)]
        e_w_used = [sem(f"e_w_used{i}") for i in range(6)]
        e_P_ready = sem("e_P_ready")
        e_X_filled = sem("e_X_filled")
        e_X_read = sem("e_X_read")
        e_gu_filled = sem("e_gu_filled")
        e_silu_ready = sem("e_silu_ready")
        e_act_ready = sem("e_act_ready")
        e_y_filled = sem("e_y_filled")
        e_y_read = sem("e_y_read")
        e_acc_open = sem("e_acc_open")
        e_done = sem("e_done")
        fin_ready = sem("fin_ready")
        stored = sem("stored")
        block = ctx.enter_context(nc.Block())

        NCONST = 8
        SMALL_LOADS = 14

        def heads_of(g):
            return [4 * (g // 2) + g % 2, 4 * (g // 2) + g % 2 + 2]

        def job_bank(key, name):
            return psum[:, (JOB[key + (name,)] - 1) % NB, :]

        def piece_source(what, c0, n):
            if what[:-1].endswith("_gain"):
                return a[what.split("_")[0] + "_norm_g"][int(what[-1]):int(what[-1]) + 1, :].to_broadcast([P, D])
            if what == "mix_gain":
                return a["norm_mix_g_2"].to_broadcast([P, D])
            if what == "moe_gain":
                return a["norm_ffn_g_2"].to_broadcast([P, D])
            w = {"w_down": a["mla_w_down"], "w_uq": a["mla_w_uq"], "w_ukv": a["mla_w_ukv"], "mla_w_o": a["mla_w_o"],
                 "gla_w_in": a["gla_w_in"], "gla_w_o": a["gla_w_o"], "w_in_2": a["w_in_2"],
                 "w_conv_out": a["w_conv_out_2"], "w_att_out": a["w_att_out_2"], "w_out": a["w_out_2"],
                 "w_router": a["w_router"]}.get(what)
            if w is None:
                w = a["peer_w_query"][int(what[-1])]
            return w[:, c0:c0 + n].rearrange("(k p) n -> p k n", p=P)

        def piece_view(n):
            _, (what, c0, cols, _) = PIECES[n]
            if "gain" in what:
                return ring[:, n % NW, 0:D]
            k = {"w_uq": QR // P, "w_ukv": KVR // P}.get(what, KD)
            return ring[:, n % NW, 0:k * cols].rearrange("p (k n) -> p k n", k=k)

        def e_slot(s):
            if s < NW:
                base = ring[:, s, :]
            else:
                base = rows[:, (s - NW) * KD * BANK:(s - NW + 1) * KD * BANK]
            if s % 3 == 2:
                return base.rearrange("p (k n) -> p k n", k=F // P)
            return base.rearrange("p (k n) -> p k n", k=KD)

        @block.sync
        def _(sp):
            for t in range(NT):
                sp.dma_start(h[:, t, :], a["x"][t * P:(t + 1) * P, :]).then_inc(loaded, 16)
            for dst, src in ((pos_i[:, :], a["positions"]),
                             (lat_gain[:, 0:QR], a["mla_g_q_lat"].to_broadcast([P, QR])),
                             (lat_gain[:, QR:], a["mla_g_kv_lat"].to_broadcast([P, KVR])),
                             (qn_gain[:, :], a["mla_g_qn"].to_broadcast([P, QK])),
                             (kn_gain[:, :], a["mla_g_kn"].to_broadcast([P, QK])),
                             (on_gain[:, :], a["gla_g_on"].to_broadcast([P, GDV])),
                             (b_gate[:, :], a["gla_b_g"]),
                             (w_g2[:, :], a["gla_w_g2"]),
                             (sub_keys[:, :, :], a["sub_keys"]),
                             (conv_w[:, :, :], a["conv_w_2"]),
                             (conv_b[:, :], a["conv_b_2"]),
                             (b_forget[:, :], a["b_forget_2"])):
                sp.dma_start(dst, src).then_inc(loaded, 16)
            for n, (key, (what, c0, cols, last)) in enumerate(PIECES):
                if n >= NW:
                    old_key, old = PIECES[n - NW]
                    sp.wait_ge(emptied, JOB[old_key + (old[3],)])
                sp.dma_start(piece_view(n), piece_source(what, c0, cols)).then_inc(weights[n % NW], 16)

            sp.wait_ge(emptied, JOB[("moe", 0, "r1")])
            sp.dma_start(fin_gain, a["norm_final_g_2"].to_broadcast([P, D])).then_inc(fin_ready, 16)

            def load_pair(r, i):
                for s in range(6):
                    sp.wait_ge(e_w_used[s], i + 1 + r * PAIRS)
                    w = (a["w_e_gate_2"], a["w_e_up_2"], a["w_e_down_2"])[s % 3]
                    src = w[bass.ds(2 * i + s // 3, 1), :, :].rearrange("e (k p) n -> p (e k) n", p=P)
                    sp.dma_start(e_slot(s), src).then_inc(e_w[s], 16)
            with sp.Fori(0, PAIRS) as i:
                load_pair(0, i)
            sp.wait_ge(dve_step, STEP["dve"][("moe", 0, "keys")])
            most = sp.value_load(e_cnt_i[0:1, 0:1], min_val=0, max_val=S)
            for r in range(1, ROUNDS):
                with sp.If(most > r * SLOTS):
                    with sp.Fori(0, PAIRS) as i:
                        load_pair(r, i)
            sp.wait_ge(fin_ready, 17)
            sp.dma_start(out.rearrange("(t p) d -> p t d", p=P), e_out).then_inc(stored, 16)
            sp.wait_ge(stored, 16)

        @block.gpsimd
        def _(pool):
            pool.memset(ident[:], 0.0)
            pool.memset(causal[:], 0.0)
            pool.memset(ones[:], 1.0)
            pool.memset(before[:], 1.0)
            pool.memset(chunk_causal[:], 1.0)
            for j in range(HALF):
                pool.memset(inv_freq[:, j:j + 1], float(np.float32(10000.0) ** np.float32(-j / HALF)))
            pool.iota(iota16[:], [[1, PK]], base=0, channel_multiplier=0, allow_small_or_imprecise_dtypes=True)
            pool.iota(iota64[:], [[1, SLOTS]], base=0, channel_multiplier=0, allow_small_or_imprecise_dtypes=True)
            pool.memset(zeros[:], 0.0).then_inc(const_ready, 1)
            pool.wait_ge(const_ready, 1)
            pool.affine_select(out=ident[:], in_=ident[:], compare_op=ALU.not_equal, fill=1.0, base=0,
                               pattern=[[-1, P]], channel_multiplier=1)
            pool.affine_select(out=causal[:], in_=causal[:], compare_op=ALU.is_ge, fill=NEG, base=0,
                               pattern=[[-1, P]], channel_multiplier=1)
            pool.affine_select(out=before[:], in_=before[:], compare_op=ALU.is_gt, fill=0.0, base=0,
                               pattern=[[1, P]], channel_multiplier=-1)
            second = junk[:, 0:CH]
            pool.affine_select(out=chunk_causal[:], in_=chunk_causal[:], compare_op=ALU.is_ge, fill=0.0, base=0,
                               pattern=[[1, CH]], channel_multiplier=-1)
            pool.affine_select(out=second, in_=ones[:, 0:CH], compare_op=ALU.is_ge, fill=0.0, base=CH,
                               pattern=[[1, CH]], channel_multiplier=-1).then_inc(const_ready, 1)
            pool.wait_ge(const_ready, 2)
            pool.affine_select(out=second, in_=second, compare_op=ALU.is_ge, fill=0.0, base=-CH,
                               pattern=[[0, CH]], channel_multiplier=1).then_inc(const_ready, 1)
            pool.wait_ge(const_ready, 3)
            pool.tensor_tensor(chunk_causal[:], chunk_causal[:], second, ALU.add).then_inc(const_ready, 1)

            def gather(g):
                b, l = g % 2, g // 2
                pool.wait_ge(dve_step, STEP["dve"][("route", g, "ready")])

                def copy_list(dst, par, head, n):
                    pool.tensor_copy(dst[:, par, :], idx[:, b, bass.ds(head * PK, PK)]).then_inc(listed, 1)
                    pool.wait_ge(listed, n)
                    pool.sem_inc(granted, 1)

                def fetch_u(head, par, r):
                    pool.wait_ge(u_used, g * P + head * PK + r + 1)
                    pool.sem_inc(granted, 1)
                    pool.indirect_dma_start(out=u_rows[:, r % RU, :], out_offset=None, in_=a["peer_u"][l],
                                            in_offset=bass.IndirectOffsetOnAxis(ap=list_u[:, par, r:r + 1], axis=0)
                                            ).then_inc(u_here[r % RU], 16)

                def fetch_v(head, par, r):
                    pool.wait_ge(v_used, g * P + head * PK + r + 1)
                    pool.sem_inc(granted, 1)
                    pool.indirect_dma_start(out=v_rows[:, r % RV, :], out_offset=None, in_=a["peer_v"][l],
                                            in_offset=bass.IndirectOffsetOnAxis(ap=list_v[:, par, r:r + 1], axis=0)
                                            ).then_inc(v_here[r % RV], 16)

                def heads(ju, jv, pu, pv, n):
                    copy_list(list_u, pu, ju, n + 1)
                    copy_list(list_v, pv, jv, n + 2)
                    for r in range(PK):
                        fetch_u(ju, pu, r)
                        fetch_v(jv, pv, r)

                n0 = g * 2 * PH
                copy_list(list_u, 0, 0, n0 + 1)
                for r in range(PK):
                    fetch_u(0, 0, r)
                with pool.Fori(0, PH // 2 - 1) as i:
                    heads(2 * i + 1, 2 * i, 1, 0, n0 + 1 + i * 4)
                    heads(2 * i + 2, 2 * i + 1, 0, 1, n0 + 3 + i * 4)
                heads(PH - 1, PH - 2, 1, 0, n0 + 13)
                copy_list(list_v, 1, PH - 1, n0 + 16)
                for r in range(PK):
                    fetch_v(PH - 1, 1, r)

            for g in range(4):
                gather(g)

        @block.vector
        def _(dve):
            links = [0]

            def link(ins):
                links[0] += 1
                ins.then_inc(dve_link, 1)
                dve.wait_ge(dve_link, links[0])

            def V(name, key):
                dve.sem_inc(dve_step, 1)
                done_names.append(key + (name,))

            done_names = []
            V_ = nc.vector

            last_got = [0]

            def got(key, name):
                last_got[0] = JOB[key + (name,)]
                quarters.upto(last_got[0] - 1)
                dve.wait_ge(emptied, last_got[0])

            def act_got(key, name, job):
                quarters.upto(JOB[key + (job,)])
                dve.wait_ge(act_step, STEP["act"][key + (name,)])

            def tick():
                quarters.tick(last_got[0])

            def rstd(col, n, count):
                s = small[:, col:col + n]
                link(V_.tensor_scalar(s, s, 1.0 / count, EPS, ALU.mult, ALU.add))
                y, half = small[:, 80:80 + n], small[:, 100:100 + n]
                link(V_.tensor_scalar(half.bitcast(i32), s.bitcast(i32), 1, None, ALU.logical_shift_right))
                link(V_.tensor_scalar(y.bitcast(i32), half.bitcast(i32), -1.0, float(0x5f3759df), ALU.mult, ALU.add))
                for _ in range(4):
                    link(V_.scalar_tensor_tensor(half, y, -0.5, y, ALU.mult, ALU.mult))
                    link(V_.tensor_tensor(half, half, s, ALU.mult))
                    link(V_.scalar_tensor_tensor(y, half, 1.5, y, ALU.add, ALU.mult))
                link(V_.tensor_copy(s, y))

            def norm(src, dst, gain):
                link(V_.tensor_tensor_reduce(out=junk[:], in0=src, in1=src, scale=1.0, scalar=0.0, op0=ALU.mult,
                                             op1=ALU.add, accum_out=small[:, 0:1]))
                rstd(0, 1, D)
                link(V_.scalar_tensor_tensor(dst, src, small[:, 0:1], gain, ALU.mult, ALU.mult))

            piece = [0]

            def gain_piece():
                n = next(i for i in range(piece[0], len(PIECES)) if "gain" in PIECES[i][1][0])
                piece[0] = n + 1
                dve.wait_ge(weights[n % NW], 16 * (n // NW + 1))
                return piece_view(n)

            def attend(key, t, Sb):
                w = (t + 1) * P

                def first(g):
                    s = Sb[:, g % 2, 0:2 * w].rearrange("p (a w) -> p a w", a=2)
                    mx = small[:, 8 + 4 * (g % 2):10 + 4 * (g % 2)]
                    got(key, f"S{t}_{g}")
                    link(V_.tensor_tensor(s[:, :, t * P:w], s[:, :, t * P:w], causal[:].unsqueeze(1).to_broadcast([P, 2, P]), ALU.add))
                    link(V_.tensor_reduce(mx, s, X, ALU.max))
                    link(V_.tensor_tensor(s, s, mx.unsqueeze(2).to_broadcast([P, 2, w]), ALU.subtract))
                    V(f"m{t}_{g}", key)

                def second(g):
                    s = Sb[:, g % 2, 0:2 * w].rearrange("p (a w) -> p a w", a=2)
                    den = small[:, 10 + 4 * (g % 2):12 + 4 * (g % 2)]
                    act_got(key, f"e{t}_{g}", f"O{t}_{g - 2}" if g >= 2 else f"S{t}_1")
                    link(V_.tensor_reduce(den, s, X, ALU.add))
                    link(V_.reciprocal(den, den))
                    link(V_.tensor_tensor(s, s, den.unsqueeze(2).to_broadcast([P, 2, w]), ALU.mult))
                    V(f"p{t}_{g}", key)

                first(0)
                for g in range(H // 2):
                    if g + 1 < H // 2:
                        first(g + 1)
                    second(g)

            def mla(t):
                key = ("mla", t)
                norm(h[:, t, :], xn, gain_piece())
                V("xn", key)
                tr, pf = m_trig, small[:, 16:17]
                ang, kk = tr[:, 0, :], tr[:, 1, :]
                link(V_.tensor_copy(pf, pos_i[:, t:t + 1]))
                link(V_.tensor_scalar(ang, inv_freq[:], pf, None, ALU.mult))
                link(V_.tensor_scalar(kk, ang, float(1 / (2 * np.pi)), 0.0, ALU.mult, ALU.add))
                ki = tr[:, 2, :].bitcast(i32)
                link(V_.tensor_copy(ki, kk))
                link(V_.tensor_copy(kk, ki))
                c1 = 6.28125
                c2 = float(np.float32(2 * np.pi - c1))
                c2h = float(np.round(c2 * 2 ** 21) / 2 ** 21)
                for c in (c1, c2h, float(2 * np.pi - c1 - c2h)):
                    link(V_.scalar_tensor_tensor(ang, kk, -c, ang, ALU.mult, ALU.add))
                lim = 3.1415925
                link(V_.tensor_scalar(tr[:, 3, :], ang, float(np.pi / 2), None, ALU.add))
                link(V_.tensor_scalar(kk, tr[:, 3, :], float(np.pi), float(-2 * np.pi), ALU.is_gt, ALU.mult))
                link(V_.tensor_tensor(kk, kk, tr[:, 3, :], ALU.add))
                link(V_.tensor_scalar(tr[:, 0:2, :], tr[:, 0:2, :], lim, -lim, ALU.min, ALU.max))
                V("cos_arg", key)
                got(key, "down1")
                for c, (o, n) in enumerate(((0, QR), (QR, KVR))):
                    link(V_.tensor_tensor_reduce(out=junk[:, 0:n], in0=m_lat[:, o:o + n], in1=m_lat[:, o:o + n],
                                                 scale=1.0, scalar=0.0, op0=ALU.mult, op1=ALU.add,
                                                 accum_out=small[:, 2 + c:3 + c]))
                    rstd(2 + c, 1, n)
                    link(V_.scalar_tensor_tensor(m_lat[:, o:o + n], m_lat[:, o:o + n], small[:, 2 + c:3 + c],
                                                 lat_gain[:, o:o + n], ALU.mult, ALU.mult))
                V("lat", key)
                got(key, "kv3")
                link(V_.tensor_copy(m_k[:, :, NOPE:QK], m_lat[:, QR + KVR:].unsqueeze(1).to_broadcast([P, H, ROPE])))
                act_got(key, "trig", "x1")
                sin = m_trig[:, 2, :].unsqueeze(1).to_broadcast([P, H, HALF])
                cos = m_trig[:, 3, :].unsqueeze(1).to_broadcast([P, H, HALF])
                for x, g in ((m_q, qn_gain), (m_k, kn_gain)):
                    ss = small[:, 20:20 + H]
                    link(V_.tensor_tensor(m_sq, x, x, ALU.mult))
                    link(V_.tensor_reduce(ss, m_sq, X, ALU.add))
                    tick()
                    rstd(20, H, QK)
                    link(V_.tensor_tensor(x, x, ss.unsqueeze(2).to_broadcast([P, H, QK]), ALU.mult))
                    tick()
                    link(V_.tensor_tensor(x, x, g[:].unsqueeze(1).to_broadcast([P, H, QK]), ALU.mult))
                    x1, x2 = x[:, :, NOPE:NOPE + HALF], x[:, :, NOPE + HALF:QK]
                    t1, t2, t3, t4 = (m_rope[:, i] for i in range(4))
                    V_.tensor_tensor(t1, x1, cos, ALU.mult)
                    V_.tensor_tensor(t2, x2, sin, ALU.mult)
                    V_.tensor_tensor(t3, x2, cos, ALU.mult)
                    link(V_.tensor_tensor(t4, x1, sin, ALU.mult))
                    V_.tensor_tensor(x1, t1, t2, ALU.subtract)
                    link(V_.tensor_tensor(x2, t3, t4, ALU.add))
                V("qk", key)
                attend(key, t, m_S)
                got(key, "out1")
                link(V_.tensor_tensor(h[:, t, :], h[:, t, :], xn, ALU.add))
                V("resid", key)

            def top16(vals, idxs, src):
                link(V_.max(vals[:, 0:8], src))
                link(V_.max_index(idxs[:, 0:8], vals[:, 0:8], src))
                link(V_.match_replace(src, vals[:, 0:8], src, -3e38))
                link(V_.max(vals[:, 8:16], src))
                link(V_.max_index(idxs[:, 8:16], vals[:, 8:16], src))

            def route(v):
                key, b, t = ("route", v), v % 2, v % 2
                if v >= 2:
                    dve.wait_ge(experts_added, v - 1)
                norm(h[:, t, :], px[:, b, :], gain_piece())
                V("xn", key)
                ru, rp = r_idx.bitcast(u32), r_pos.bitcast(u32)
                for i in range(2 * PH):
                    if i % 8 == 0:
                        got(key, f"s{i // 4 + 1}")
                    top16(r_val[:, i, :], ru[:, i, :], r_S[:, i, :])
                    if i > 8 and i % 3 == 0:
                        tick()
                link(V_.tensor_copy(r_idf, ru))
                val = r_val.rearrange("p (h c) k -> p h c k", c=2)
                c4 = r_c.rearrange("p h (a b) -> p h a b", a=PK)
                t4 = r_t.rearrange("p h (a b) -> p h a b", a=PK)
                full = [P, PH, PK, PK]
                link(V_.tensor_tensor(c4, val[:, :, 0, :].unsqueeze(3).to_broadcast(full),
                                      val[:, :, 1, :].unsqueeze(2).to_broadcast(full), ALU.add))
                for i in range(PH):
                    if i % 3 == 0:
                        tick()
                    top16(r_best[:, i, :], rp[:, i, :], r_c[:, i, :])
                gt = gate[:, b, :].rearrange("p (h k) -> p h k", h=PH)
                link(V_.tensor_tensor(gt, r_best, r_best[:, :, 0:1].to_broadcast([P, PH, PK]), ALU.subtract))
                V("shift", key)
                ai = r_ab.bitcast(i32)
                rpi = r_pos.bitcast(i32).rearrange("p h k -> p (h k)")
                link(V_.tensor_scalar(ai[:, 0, :], rpi, 4, None, ALU.logical_shift_right))
                link(V_.tensor_scalar(ai[:, 1, :], rpi, 15, None, ALU.bitwise_and))
                link(V_.tensor_copy(r_sel, ai))
                idf = r_idf.rearrange("p (h c) k -> p h c k", c=2)
                for c in range(2):
                    ab = r_sel[:, c, :].rearrange("p (h k) -> p h k", h=PH)
                    link(V_.tensor_tensor(t4, ab.unsqueeze(3).to_broadcast(full),
                                          iota16[:].unsqueeze(1).unsqueeze(1).to_broadcast(full), ALU.is_equal))
                    tick()
                    link(V_.tensor_tensor(t4, t4, idf[:, :, c, :].unsqueeze(2).to_broadcast(full), ALU.mult))
                    tick()
                    link(V_.tensor_reduce(r_ab[:, c, :].rearrange("p (h k) -> p h k", h=PH), t4, X, ALU.add))
                link(V_.scalar_tensor_tensor(r_sel[:, 0, :], r_ab[:, 0, :], float(NKEYS), r_ab[:, 1, :], ALU.mult, ALU.add))
                link(V_.tensor_copy(idx[:, b, :], r_sel[:, 0, :]))
                act_got(key, "exp", "s3")
                den = small[:, 40:40 + PH]
                link(V_.tensor_reduce(den, gt, X, ALU.add))
                link(V_.reciprocal(den, den))
                link(V_.tensor_tensor(gt, gt, den.unsqueeze(2).to_broadcast([P, PH, PK]), ALU.mult))
                V("ready", key)

            def experts(g, j, q):
                b = g % 2
                if j < PH:
                    for r in range(q * QUART, (q + 1) * QUART):
                        n = g * P + j * PK + r
                        dve.wait_ge(u_here[n % RU], 16 * (n // RU + 1))
                        dve.wait_ge(u_used, n + RU)
                        V_.tensor_tensor_reduce(out=junk[:], in0=u_rows[:, n % RU, :], in1=px[:, b, :], scale=1.0,
                                                scalar=0.0, op0=ALU.mult, op1=ALU.add,
                                                accum_out=hid[:, j * PK + r:j * PK + r + 1]).then_inc(u_used, 1)
                    dve.wait_ge(u_used, n + 1 + RU)
                if j >= 1 and q == 0:
                    c = slice((j - 1) * PK, j * PK)
                    dve.wait_ge(gelu_ready, g * PH + j)
                    V_.tensor_tensor(wgt[:, c], gel[:, c], gate[:, b, c], ALU.mult).then_inc(wgt_ready, 1)

            quarters = Quarters(experts)

            def experts_end(g):
                t = g % 2
                dve.wait_ge(v_used, (g + 1) * P + RV)
                V_.tensor_tensor(h[:, t, :], h[:, t, :], psum[:, 6:8, :].rearrange("p a b -> p (a b)"),
                                 ALU.add).then_inc(experts_added, 1)
                dve.wait_ge(experts_added, g + 1)

            def log_sigmoid_abs(z, e):
                link(V_.scalar_tensor_tensor(e, z, -1.0, z, ALU.mult, ALU.max))

            def gla(t):
                key = ("gla", t)
                if t == 0:
                    link(V_.memset(g_state, 0.0))
                norm(h[:, t, :], xn, gain_piece())
                V("xn", key)
                got(key, "gate")
                log_sigmoid_abs(g_z, g_e)
                V("abs", key)
                act_got(key, "ln", "gate")
                link(V_.scalar_tensor_tensor(g_z, g_z, 0.0, g_e, ALU.min, ALU.subtract))
                link(V_.tensor_scalar(g_z, g_z, 1.0 / TAU, None, ALU.mult))
                for hh in range(GH):
                    for c in range(2):
                        cs = slice(c * CH, (c + 1) * CH)
                        last = V_.tensor_tensor_scan(g_b[:, hh, cs], ones[:, 0:CH], g_z[:, hh, cs], 0.0, ALU.mult, ALU.add)
                link(last)
                V("b", key)
                act_got(key, "eb", "gate")
                V_.tensor_tensor(g_qT, g_qT, g_eb, ALU.mult)
                link(V_.tensor_tensor(g_enb, g_kT, g_enb, ALU.mult))
                V("qd", key)
                act_got(key, "ekd", "gate")
                link(V_.tensor_tensor(g_kd, g_kT, g_kd, ALU.mult))
                V("kd", key)
                got(key, "at")
                link(V_.scalar_tensor_tensor(g_at, g_at, 3e38, chunk_causal[:].unsqueeze(1).to_broadcast([P, GH, CH]),
                                             ALU.min, ALU.mult))
                V("at", key)
                got(key, "kv01")
                kv = g_kv.rearrange("p c (h v) -> p c h v", h=GH)
                for hh in range(GH):
                    last = V_.scalar_tensor_tensor(g_mid[:, hh, :], g_state[:, hh, :], g_eb[:, hh, CH - 1:CH], kv[:, 0, hh, :],
                                                   ALU.mult, ALU.add)
                link(last)
                V("state1", key)
                got(key, "o1")
                o3 = g_o.rearrange("p (h v) -> p h v", h=GH)
                sq = xn.rearrange("p (h v) -> p h v", h=GH)
                ss = small[:, 50:50 + GH]
                link(V_.tensor_tensor(sq, o3, o3, ALU.mult))
                link(V_.tensor_reduce(ss, sq, X, ALU.add))
                rstd(50, GH, GDV)
                tick()
                link(V_.tensor_tensor(o3, o3, ss.unsqueeze(2).to_broadcast([P, GH, GDV]), ALU.mult))
                link(V_.tensor_tensor(o3, o3, on_gain[:].unsqueeze(1).to_broadcast([P, GH, GDV]), ALU.mult))
                link(V_.tensor_tensor(g_o, g_o, g_r, ALU.mult))
                V("on", key)
                for hh in range(GH):
                    last = V_.scalar_tensor_tensor(g_state[:, hh, :], g_mid[:, hh, :], g_eb[:, hh, P - 1:P], kv[:, 1, hh, :],
                                                   ALU.mult, ALU.add)
                link(last)
                V("state2", key)
                got(key, "out1")
                link(V_.tensor_tensor(h[:, t, :], h[:, t, :], xn, ALU.add))
                V("resid", key)

            def mix(v):
                key = ("mix", 0)
                gain = gain_piece()
                for t in range(NT):
                    if t:
                        got(key, "x01")
                    norm(h[:, t, :], x_xn, gain)
                    V(f"xn{t}", key)
                V_.memset(x_z[:, :, 0:2], 0.0)
                got(key, "cu3")
                link(V_.tensor_tensor(x_z[:, :, 2:], x_cc, x_gc, ALU.mult))
                for c in range(KD):
                    link(V_.tensor_scalar(x_cc[:, c, :], x_z[:, c, 0:S], conv_w[:, 0, c:c + 1], conv_b[:, c:c + 1], ALU.mult, ALU.add))
                    for i in (1, 2):
                        link(V_.scalar_tensor_tensor(x_cc[:, c, :], x_z[:, c, i:i + S], conv_w[:, i, c:c + 1], x_cc[:, c, :],
                                                     ALU.mult, ALU.add))
                got(key, "f")
                link(V_.scalar_tensor_tensor(x_nf_(), x_f[0:FH], -1.0, x_f[0:FH], ALU.mult, ALU.max))
                V("abs", key)
                act_got(key, "ln", "f")
                link(V_.scalar_tensor_tensor(x_f[0:FH], x_f[0:FH], 0.0, x_nf_(), ALU.min, ALU.subtract))
                link(V_.tensor_tensor_scan(x_cum[0:FH, 0:P], ones[0:FH, :], x_f[0:FH, 0:P], 0.0, ALU.mult, ALU.add))
                link(V_.tensor_tensor_scan(x_cum[0:FH, P:S], ones[0:FH, :], x_f[0:FH, P:S], x_cum[0:FH, P - 1:P],
                                           ALU.mult, ALU.add))
                link(V_.tensor_scalar(x_ncum[0:FH], x_cum[0:FH], -1.0, None, ALU.mult))
                V("cum", key)
                attend(key, 0, x_S)
                attend(key, 1, x_S)
                link(V_.tensor_tensor(x_cb, x_cb, x_cc, ALU.mult))
                V("convy", key)
                got(key, "ya3")
                V_.tensor_tensor(x_yc, x_yc, x_gc, ALU.mult)
                link(V_.tensor_tensor(x_ya, x_ya, x_ga, ALU.mult))
                link(V_.tensor_tensor(x_yc, x_yc, x_ya, ALU.add))
                V("m", key)
                got(key, "o11")
                link(V_.tensor_tensor(h[:, :, :], h[:, :, :], x_v, ALU.add))
                V("resid", key)

            def x_nf_():
                return x_xn[0:FH, 0:S]

            def moe(v):
                key = ("moe", 0)
                gain = gain_piece()
                for t in range(NT):
                    norm(h[:, t, :], hn[:, t, :], gain)
                    V(f"xn{t}", key)
                link(V_.memset(e_pg, -1.0))
                got(key, "r1")
                lg = e_lg[:, :, 0:NG]
                g4 = e_pg[:, :, 0:NG]
                mx, den, gv = small[:, 60:62], small[:, 62:64], small[:, 64:66]
                link(V_.tensor_reduce(mx, lg, X, ALU.max))
                link(V_.tensor_tensor(g4, lg, mx.unsqueeze(2).to_broadcast([P, NT, NG]), ALU.subtract))
                V("gshift", key)
                act_got(key, "gexp", "r1")
                link(V_.tensor_reduce(den, g4, X, ALU.add))
                link(V_.reciprocal(den, den))
                link(V_.tensor_tensor(g4, g4, den.unsqueeze(2).to_broadcast([P, NT, NG]), ALU.mult))
                le = e_lg[:, :, NG:].rearrange("p t (g e) -> p t g e", g=NG)
                iota8 = iota16[:, 0:8]
                gi = e_tmp[:, 0, 0:8].bitcast(u32)
                for t in range(NT):
                    link(V_.max(e_top[:, t, :], e_pg[:, t, :]))
                    link(V_.tensor_copy(gv[:, t:t + 1], e_top[:, t, 0:1]))
                    link(V_.max_index(gi, e_top[:, t, :], e_pg[:, t, :]))
                    link(V_.tensor_copy(e_tmp[:, 1, 0:1], gi[:, 0:1]))
                    link(V_.tensor_scalar(e_oh[:, t, :], iota8, e_tmp[:, 1, 0:1], None, ALU.is_equal))
                    link(V_.tensor_scalar(e_pe[:, t, :], le[:, t, 0, :], e_oh[:, t, 0:1], None, ALU.mult))
                    for g in range(1, NG):
                        link(V_.scalar_tensor_tensor(e_pe[:, t, :], le[:, t, g, :], e_oh[:, t, g:g + 1], e_pe[:, t, :],
                                                     ALU.mult, ALU.add))
                link(V_.tensor_reduce(mx, e_pe, X, ALU.max))
                link(V_.tensor_tensor(e_pe, e_pe, mx.unsqueeze(2).to_broadcast([P, NT, EPG]), ALU.subtract))
                V("eshift", key)
                act_got(key, "eexp", "r1")
                link(V_.tensor_reduce(den, e_pe, X, ALU.add))
                link(V_.reciprocal(den, den))
                link(V_.tensor_tensor(e_pe, e_pe, den.unsqueeze(2).to_broadcast([P, NT, EPG]), ALU.mult))
                for t in range(NT):
                    link(V_.max(e_top[:, t, :], e_pe[:, t, :]))
                    link(V_.max_index(gi, e_top[:, t, :], e_pe[:, t, :]))
                    link(V_.tensor_copy(e_tmp[:, 1, 0:2], gi[:, 0:2]))
                    sm = small[:, 66:67]
                    link(V_.tensor_tensor(sm, e_top[:, t, 0:1], e_top[:, t, 1:2], ALU.add))
                    link(V_.reciprocal(sm, sm))
                    link(V_.tensor_tensor(sm, sm, gv[:, t:t + 1], ALU.mult))
                    link(V_.tensor_scalar(e_top[:, t, 0:2], e_top[:, t, 0:2], sm, None, ALU.mult))
                    w8, a8, x8 = e_tmp[:, 2, 0:8], e_tmp[:, 2, 8:16], e_tmp[:, 2, 16:24]
                    link(V_.tensor_scalar(a8, iota8, e_tmp[:, 1, 0:1], None, ALU.is_equal))
                    link(V_.tensor_scalar(x8, iota8, e_tmp[:, 1, 1:2], None, ALU.is_equal))
                    link(V_.tensor_scalar(w8, a8, e_top[:, t, 0:1], None, ALU.mult))
                    link(V_.scalar_tensor_tensor(w8, x8, e_top[:, t, 1:2], w8, ALU.mult, ALU.add))
                    link(V_.tensor_tensor(a8, a8, x8, ALU.add))
                    for g in range(NG):
                        V_.tensor_scalar(e_A[:, t, g * EPG:(g + 1) * EPG], a8, e_oh[:, t, g:g + 1], None, ALU.mult)
                        last = V_.tensor_scalar(e_W[:, t, g * EPG:(g + 1) * EPG], w8, e_oh[:, t, g:g + 1], None, ALU.mult)
                    link(last)
                V("picked", key)
                got(key, "rank")
                rk = e_rank[:, 0:NT, :]
                tmp = e_tmp[:, 0:NT, :]
                link(V_.tensor_scalar(tmp, e_A, -1000.0, 1000.0, ALU.mult, ALU.add))
                link(V_.tensor_tensor(rk, rk, tmp, ALU.add))
                for r in range(ROUNDS):
                    last = V_.tensor_scalar(e_key[:, r, :].rearrange("p (t e) -> p t e", t=NT), rk, float(-r * SLOTS), None, ALU.add)
                link(last)
                link(V_.tensor_reduce(e_cnt[:, 0:1], e_rank[:, NT, :], X, ALU.max))
                link(V_.tensor_copy(e_cnt_i[:, 0:1], e_cnt[:, 0:1]))
                V("keys", key)

                def pair(r, i):
                    n = r * PAIRS + i
                    dve.wait_ge(e_X_read, 3 * n + 3)
                    for t in range(NT):
                        for e in range(2):
                            col = t * NE + 2 * i + e
                            k = e_key[:, r, bass.ds(col, 1)]
                            w = e_W.rearrange("p t e -> p (t e)")[:, bass.ds(col, 1)]
                            cs = slice(e * SLOTS, (e + 1) * SLOTS)
                            V_.tensor_scalar(e_P[:, t, cs], iota64[:], k, None, ALU.is_equal)
                            last = V_.tensor_scalar(e_Pw[:, t, cs], iota64[:], k, w, ALU.is_equal, ALU.mult)
                    last.then_inc(e_P_ready, 1)
                    for e in range(2):
                        dve.wait_ge(e_silu_ready, 2 * n + e + 1)
                        V_.tensor_tensor(e_act[:, e].rearrange("p j s -> p (j s)"), e_silu[:, e, :], psum[:, 5 - e, 4 * SLOTS:8 * SLOTS],
                                         ALU.mult).then_inc(e_act_ready, 1)

                with dve.Fori(0, PAIRS) as i:
                    pair(0, i)
                most = dve.value_load(e_cnt_i[0:1, 0:1], min_val=0, max_val=S)
                for r in range(1, ROUNDS):
                    with dve.If(most > r * SLOTS):
                        with dve.Fori(0, PAIRS) as i:
                            pair(r, i)
                dve.wait_ge(e_done, 1)
                link(V_.tensor_tensor(h[:, :, :], h[:, :, :], psum[:, 0:4, :].rearrange("p (t a) b -> p t (a b)", t=NT), ALU.add))
                dve.wait_ge(fin_ready, 16)
                norm(h[:, 0, :], e_out[:, 0, :], fin_gain)
                norm(h[:, 1, :], e_out[:, 1, :], fin_gain)
                dve.sem_inc(fin_ready, 1)

            dve.sem_inc(u_used, RU)
            dve.wait_ge(const_ready, 4)
            dve.wait_ge(loaded, 16 * SMALL_LOADS)
            run = {"mla": mla, "route": route, "gla": gla, "mix": mix, "moe": moe}
            for stage, v in BEFORE:
                run[stage](v)
            for g, beside in enumerate(BESIDE):
                quarters.open(g)
                for stage, v in beside:
                    run[stage](v)
                quarters.close()
                experts_end(g)
            for stage, v in AFTER:
                run[stage](v)
            assert done_names == list(STEP["dve"]), [x for x in zip(done_names, STEP["dve"]) if x[0] != x[1]][:2]

        @block.scalar
        def _(act):
            A_ = nc.scalar
            done_jobs, done_steps, links = [], [], [0]

            def empty(key, name, *moves):
                act.wait_ge(filled, JOB[key + (name,)])
                for dst, src, func, scale, bias in moves:
                    last = A_.activation(dst, src, func, scale=scale, bias=bias) if bias is not None else \
                        A_.activation(dst, src, func, scale=scale)
                last.then_inc(emptied, 1)
                done_jobs.append(key + (name,))
                quarters.upto(JOB[key + (name,)])

            def copy(key, name, dst, cols=None, scale=1.0, func=ACT.Copy, parts=P):
                src = job_bank(key, name)
                if cols is not None:
                    src = src[:, 0:cols]
                src = src[0:parts]
                n = len(dst.shape)
                if n == 3:
                    src = src.rearrange("p (a b) -> p a b", a=dst.shape[1])
                empty(key, name, (dst, src, func, scale, None))

            def seen(key, name):
                act.wait_ge(dve_step, STEP["dve"][key + (name,)])

            def A(name, key, last):
                last.then_inc(act_step, 1)
                done_steps.append(key + (name,))

            def link(ins):
                links[0] += 1
                ins.then_inc(act_link, 1)
                act.wait_ge(act_link, links[0])

            def attend(key, t, Sb, pT, oT, scale):
                w = (t + 1) * P

                def scores(g):
                    if g >= 2:
                        act.wait_ge(filled, JOB[key + (f"T{t}_{g - 2}",)])
                    copy(key, f"S{t}_{g}", Sb[:, g % 2, 0:2 * w], 2 * w, scale)

                def exps(g):
                    seen(key, f"m{t}_{g}")
                    A(f"e{t}_{g}", key, A_.activation(Sb[:, g % 2, 0:2 * w], Sb[:, g % 2, 0:2 * w], ACT.Exp))
                scores(0)
                scores(1)
                exps(0)
                for g in range(H // 2):
                    if g + 1 < H // 2:
                        exps(g + 1)
                    copy(key, f"T{t}_{g}", pT[:, g % 2, 0:2 * w], 2 * w)
                    if g + 2 < H // 2:
                        scores(g + 2)
                    half = slice((g % 2) * DV, (g % 2 + 1) * DV)
                    empty(key, f"O{t}_{g}", (oT[half, 2 * (g // 2):2 * (g // 2) + 2, :],
                                             job_bank(key, f"O{t}_{g}")[half, 0:2 * P].rearrange("p (a b) -> p a b", a=2),
                                             ACT.Copy, 1.0, None))

            def mla(t):
                key = ("mla", t)
                for i in range(2):
                    copy(key, f"x{i}", xT[:, 4 * i:4 * i + 4, :])
                seen(key, "cos_arg")
                A("trig", key, A_.activation(m_trig[:, 2:4, :], m_trig[:, 0:2, :], ACT.Sin))
                copy(key, "down0", m_lat[:, 0:BANK])
                copy(key, "down1", m_lat[:, BANK:], QR + KVR + ROPE - BANK)
                copy(key, "cq", m_cT[:, 0:3, :], 3 * P)
                copy(key, "ckv", m_cT[:, 3:5, :], 2 * P)
                for i in range(3):
                    copy(key, f"q{i}", m_q.rearrange("p h d -> p (h d)")[:, i * BANK:(i + 1) * BANK])
                for i in range(4):
                    src = job_bank(key, f"kv{i}").rearrange("p (h d) -> p h d", h=4)
                    vdst = k_V[:, t, i * 4 * DV:(i + 1) * 4 * DV].rearrange("p (h d) -> p h d", h=4)
                    empty(key, f"kv{i}", (m_k[:, 4 * i:4 * i + 4, 0:NOPE], src[:, :, 0:NOPE], ACT.Copy, 1.0, None),
                          (vdst, src[:, :, NOPE:], ACT.Copy, 1.0, None))
                for i in range(4):
                    copy(key, f"qT{i}", m_qT[0:QK, 4 * i:4 * i + 4, :], parts=QK)
                for i in range(4):
                    copy(key, f"kT{i}", k_T[0:QK, 4 * i:4 * i + 4, t * P:(t + 1) * P], parts=QK)
                attend(key, t, m_S, m_pT, m_oT, float(QK) ** -0.5)
                for i in range(2):
                    copy(key, f"out{i}", xn[:, i * BANK:(i + 1) * BANK])

            def route(v):
                key = ("route", v)
                for i in range(2):
                    copy(key, f"x{i}", xT[:, 4 * i:4 * i + 4, :])
                for i in range(2):
                    copy(key, f"q{i}", r_qT[:, 4 * i:4 * i + 4, :])
                for i in range(4):
                    halves = r_S.rearrange("p (h c) n -> p h c n", c=2)
                    copy(key, f"s{i}", halves[:, 4 * (i // 2):4 * (i // 2) + 4, i % 2, :])
                seen(key, "shift")
                A("exp", key, A_.activation(gate[:, v % 2, :], gate[:, v % 2, :], ACT.Exp))

            def experts(g, j, q):
                if j == 0:
                    return
                c = slice((j - 1) * PK, j * PK)
                if q == 0:
                    act.wait_ge(u_used, g * P + j * PK + RU)
                    A_.activation(gel[:, c], hid[:, c], ACT.Gelu).then_inc(gelu_ready, 1)
                    act.wait_ge(wgt_ready, g * PH + j)
                for r in range((j - 1) * PK + q * QUART, (j - 1) * PK + (q + 1) * QUART):
                    n = g * P + r
                    act.wait_ge(v_used, n - 3 + RV)
                    A_.activation(diag[:, n % 4, :], ident[:], ACT.Copy, scale=wgt[:, r:r + 1]).then_inc(diag_ready, 1)

            quarters = Quarters(experts)

            def gla(t):
                key = ("gla", t)
                for i in range(2):
                    copy(key, f"x{i}", xT[:, 4 * i:4 * i + 4, :])
                copy(key, "q", g_qT, scale=float(GDK) ** -0.5)
                copy(key, "k", g_kT)
                for i in range(2):
                    copy(key, f"v{i}", g_v[:, i * BANK:(i + 1) * BANK])
                for i in range(2):
                    copy(key, f"r{i}", g_r[:, i * BANK:(i + 1) * BANK], func=ACT.Silu)
                copy(key, "low", g_low[0:GR, :], P, parts=GR)
                zb = job_bank(key, "gate").rearrange("p (h t) -> p h t", h=GH)
                empty(key, "gate", *[(g_z[:, i, :], zb[:, i, :], ACT.Identity, 1.0, b_gate[:, i:i + 1]) for i in range(GH)])
                seen(key, "abs")
                last = A_.activation(g_e, g_e, ACT.Exp, scale=-1.0)
                A("exp", key, last)
                act.wait_ge(act_step, STEP["act"][key + ("exp",)])
                A("ln", key, A_.activation(g_e, g_e, ACT.Ln, bias=1.0))
                seen(key, "b")
                A_.activation(g_eb, g_b, ACT.Exp)
                A("eb", key, A_.activation(g_enb, g_b, ACT.Exp, scale=-1.0))
                for hh in range(GH):
                    for c in range(2):
                        cs = slice(c * CH, (c + 1) * CH)
                        last = A_.activation(g_kd[:, hh, cs], g_b[:, hh, cs], ACT.Exp, scale=-1.0,
                                             bias=g_b[:, hh, (c + 1) * CH - 1:(c + 1) * CH])
                A("ekd", key, last)
                copy(key, "kd", g_kdn)
                copy(key, "at", g_at, GH * CH)
                for c in range(2):
                    for i in range(2):
                        copy(key, f"kv{c}{i}", g_kv[:, c, i * BANK:(i + 1) * BANK])
                for i in range(2):
                    copy(key, f"o{i}", g_o[:, i * BANK:(i + 1) * BANK])
                for i in range(2):
                    copy(key, f"oT{i}", xT[:, 4 * i:4 * i + 4, :])
                for i in range(2):
                    copy(key, f"out{i}", xn[:, i * BANK:(i + 1) * BANK])

            def mix(v):
                key = ("mix", 0)
                for t in range(NT):
                    for i in range(2):
                        copy(key, f"x{t}{i}", x_xT[:, 4 * i:4 * i + 4, t * P:(t + 1) * P])
                for m, dst in (("cc", x_cc), ("cu", x_gc), ("cb", x_cb), ("q", x_q), ("k", x_k)):
                    for i in range(4):
                        copy(key, f"{m}{i}", dst[:, 2 * i:2 * i + 2, :], scale=(FD ** -0.5 if m == "q" else 1.0))
                for i in range(2):
                    for t in range(NT):
                        copy(key, f"v{i}{t}", x_v[:, t, i * BANK:(i + 1) * BANK])
                empty(key, "f", (x_f[0:FH], job_bank(key, "f")[0:FH, 0:S], ACT.Identity, 1.0, b_forget[:, :]))
                seen(key, "abs")
                nf = x_xn[0:FH, 0:S]
                A("exp", key, A_.activation(nf, nf, ACT.Exp, scale=-1.0))
                act.wait_ge(act_step, STEP["act"][key + ("exp",)])
                A("ln", key, A_.activation(nf, nf, ACT.Ln, bias=1.0))
                for m, dst in (("gc", x_gc), ("ga", x_ga)):
                    for i in range(4):
                        copy(key, f"{m}{i}", dst[:, 2 * i:2 * i + 2, :], func=ACT.Sigmoid)
                for t in range(NT):
                    attend(key, t, x_S, x_pT, x_oT[:, :, t * P:(t + 1) * P], 1.0)
                seen(key, "convy")
                for m, dst in (("yc", x_yc), ("ya", x_ya)):
                    for i in range(4):
                        copy(key, f"{m}{i}", dst[:, 2 * i:2 * i + 2, :])
                for i in range(2):
                    for t in range(NT):
                        copy(key, f"o{i}{t}", x_v[:, t, i * BANK:(i + 1) * BANK])

            def moe(v):
                key = ("moe", 0)
                for t in range(NT):
                    if t:
                        act.wait_ge(filled, JOB[key + ("x10",)])
                    for i in range(2):
                        copy(key, f"x{t}{i}", e_X[:, t, :].rearrange("p (k n) -> p k n", k=KD)[:, 4 * i:4 * i + 4, :])
                for t in range(NT):
                    copy(key, f"r{t}", e_lg[:, t, :], NG + NE)
                seen(key, "gshift")
                g4, e8 = e_pg[:, :, 0:NG], e_pe
                A("gexp", key, A_.activation(g4, g4, ACT.Exp))
                seen(key, "eshift")
                A("eexp", key, A_.activation(e8, e8, ACT.Exp))
                copy(key, "rank", e_rank, 3 * NE)
                link(A_.activation(e_PwT, zeros[:].unsqueeze(1).to_broadcast([P, NT, P]), ACT.Copy))
                act.sem_inc(e_X_read, 3)

                def pair(r, i):
                    n = r * PAIRS + i
                    for q in range(2):
                        act.wait_ge(e_X_filled, 3 * n + q + 1)
                        A_.activation(e_xT[:, 4 * q:4 * q + 4, :], psum[:, 4 + q, :].rearrange("p (a b) -> p a b", a=4),
                                      ACT.Copy).then_inc(e_X_read, 1)
                    act.wait_ge(e_X_filled, 3 * n + 3)
                    A_.activation(e_PwT, psum[:, 4, 0:NT * P].rearrange("p (a b) -> p a b", a=NT), ACT.Copy).then_inc(e_X_read, 1)
                    act.wait_ge(e_act_ready, 2 * n + 1)
                    for e in range(2):
                        act.wait_ge(e_gu_filled, 2 * n + e + 1)
                        A_.activation(e_silu[:, e, :], psum[:, 5 - e, 0:4 * SLOTS], ACT.Silu).then_inc(e_silu_ready, 1)
                    for c in range(2):
                        act.wait_ge(e_y_filled, 2 * n + c + 1)
                        A_.activation(e_y[:, c * BANK:(c + 1) * BANK], psum[:, 6 + c, :], ACT.Copy).then_inc(e_y_read, 1)

                act.sem_inc(e_act_ready, 1)
                act.wait_ge(dve_step, STEP["dve"][key + ("keys",)])
                with act.Fori(0, PAIRS) as i:
                    pair(0, i)
                most = act.value_load(e_cnt_i[0:1, 0:1], min_val=0, max_val=S)
                for r in range(1, ROUNDS):
                    with act.If(most > r * SLOTS):
                        with act.Fori(0, PAIRS) as i:
                            pair(r, i)

            act.wait_ge(loaded, 16 * SMALL_LOADS)
            act.wait_ge(const_ready, 4)
            run = {"mla": mla, "route": route, "gla": gla, "mix": mix, "moe": moe}
            for stage, v in BEFORE:
                run[stage](v)
            for g, beside in enumerate(BESIDE):
                quarters.open(g)
                for stage, v in beside:
                    run[stage](v)
                quarters.close()
            for stage, v in AFTER:
                run[stage](v)
            assert done_jobs == list(JOB), [x for x in zip(done_jobs, JOB) if x[0] != x[1]][:2]
            assert done_steps == list(STEP["act"]), [x for x in zip(done_steps, STEP["act"]) if x[0] != x[1]][:2]

        @block.tensor
        def _(pe):
            mm, tp = nc.tensor.matmul, nc.tensor.transpose
            done_jobs, piece = [], [0]

            def seen(key, name):
                pe.wait_ge(dve_step, STEP["dve"][key + (name,)])

            def got(key, name):
                pe.wait_ge(emptied, JOB[key + (name,)])

            def open_bank(key, name):
                n = JOB[key + (name,)]
                if n > NB:
                    pe.wait_ge(emptied, n - NB)
                return job_bank(key, name)

            def close(key, name, last):
                last.then_inc(filled, 1)
                done_jobs.append(key + (name,))
                quarters.upto(JOB[key + (name,)])

            def next_piece():
                while "gain" in PIECES[piece[0]][1][0]:
                    piece[0] += 1
                n = piece[0]
                piece[0] += 1
                pe.wait_ge(weights[n % NW], 16 * (n // NW + 1))
                return piece_view(n)

            def transposes(key, name, sources):
                bank, at = open_bank(key, name), 0
                for s in sources:
                    parts, n = s.shape[1], s.shape[0]
                    last = tp(bank[0:parts, at:at + n], s, ident[0:n, 0:n])
                    at += n
                close(key, name, last)

            def chunks(x, i):
                return [x[:, c * P:(c + 1) * P] for c in range(4 * i, 4 * i + 4)]

            def project(key, name, lhs, rhs, kn, cols):
                bank = open_bank(key, name)
                for k in range(kn):
                    last = mm(bank[:, 0:cols], lhs(k), rhs(k), start=k == 0, stop=k == kn - 1)
                close(key, name, last)

            def project_T(key, name, w, cols, x, n):
                bank = open_bank(key, name)
                for i, c0 in enumerate(cols):
                    for k in range(KD):
                        last = mm(bank[:, i * n:(i + 1) * n], w[:, k, c0:c0 + P], x[:, k, :], start=k == 0, stop=k == KD - 1)
                close(key, name, last)

            def attend(key, t, score, Sb, pT, vals):
                def scores(g):
                    bank = open_bank(key, f"S{t}_{g}")
                    w = (t + 1) * P
                    for e in range(2):
                        last = score(heads_of(g)[e], bank[:, e * w:(e + 1) * w], w)
                    close(key, f"S{t}_{g}", last)
                scores(0)
                scores(1)
                for g in range(H // 2):
                    seen(key, f"p{t}_{g}")
                    transposes(key, f"T{t}_{g}", [Sb[:, g % 2, c * P:(c + 1) * P] for c in range(2 * (t + 1))])
                    if g + 2 < H // 2:
                        scores(g + 2)
                    got(key, f"T{t}_{g}")
                    bank = open_bank(key, f"O{t}_{g}")
                    for e in range(2):
                        for kt in range(t + 1):
                            c = e * (t + 1) + kt
                            half = slice((g % 2) * DV, (g % 2 + 1) * DV)
                            last = mm(bank[half, e * P:(e + 1) * P], vals(kt, heads_of(g)[e]), pT[:, g % 2, c * P:(c + 1) * P],
                                      start=kt == 0, stop=kt == t)
                    close(key, f"O{t}_{g}", last)

            def mla(t):
                key = ("mla", t)
                seen(key, "xn")
                for i in range(2):
                    transposes(key, f"x{i}", chunks(xn, i))
                got(key, "x1")
                for i, cols in enumerate((BANK, QR + KVR + ROPE - BANK)):
                    w = next_piece()
                    project(key, f"down{i}", lambda k: xT[:, k, :], lambda k: w[:, k, :], KD, cols)
                seen(key, "lat")
                transposes(key, "cq", [m_lat[:, c * P:(c + 1) * P] for c in range(3)])
                transposes(key, "ckv", [m_lat[:, c * P:(c + 1) * P] for c in range(3, 5)])
                got(key, "cq")
                for i in range(3):
                    w = next_piece()
                    project(key, f"q{i}", lambda k: m_cT[:, k, :], lambda k: w[:, k, :], QR // P, BANK)
                got(key, "ckv")
                for i in range(4):
                    w = next_piece()
                    project(key, f"kv{i}", lambda k: m_cT[:, 3 + k, :], lambda k: w[:, k, :], KVR // P, BANK)
                seen(key, "qk")
                for i in range(4):
                    transposes(key, f"qT{i}", [m_q[:, hh, :] for hh in range(4 * i, 4 * i + 4)])
                for i in range(4):
                    transposes(key, f"kT{i}", [m_k[:, hh, :] for hh in range(4 * i, 4 * i + 4)])
                got(key, "kT3")

                def score(hh, bank, w):
                    return mm(bank, m_qT[0:QK, hh, :], k_T[0:QK, hh, 0:w], start=True, stop=True)
                attend(key, t, score, m_S, m_pT, lambda kt, hh: k_V[:, kt, hh * DV:(hh + 1) * DV])
                got(key, f"O{t}_7")
                for i in range(2):
                    w = next_piece()
                    project(key, f"out{i}", lambda k: m_oT[:, k, :], lambda k: w[:, k, :], KD, BANK)

            def route(v):
                key, b = ("route", v), v % 2
                seen(key, "xn")
                for i in range(2):
                    transposes(key, f"x{i}", chunks(px[:, b, :], i))
                got(key, "x1")
                for i in range(2):
                    project_T(key, f"q{i}", next_piece(), [c * P for c in range(4)], xT, P)
                got(key, "q1")
                for i in range(4):
                    bank = open_bank(key, f"s{i}")
                    for j in range(4):
                        hh, c = 4 * (i // 2) + j, i % 2
                        half = slice(c * 64, (c + 1) * 64)
                        last = mm(bank[:, j * P:(j + 1) * P], r_qT[half, hh, :], sub_keys[half, v // 2, :], start=True, stop=True)
                    close(key, f"s{i}", last)

            def experts(g, j, q):
                if j == 0:
                    return
                if j == 1 and q == 0 and g:
                    pe.wait_ge(experts_added, g)
                for r in range((j - 1) * PK + q * QUART, (j - 1) * PK + (q + 1) * QUART):
                    n = g * P + r
                    pe.wait_ge(v_here[n % RV], 16 * (n // RV + 1))
                    pe.wait_ge(diag_ready, n + 1)
                    for c in range(2):
                        last = mm(psum[:, 6 + c, :], diag[:, n % 4, :], v_rows[:, n % RV, c * BANK:(c + 1) * BANK],
                                  start=r == 0, stop=r == P - 1)
                    last.then_inc(v_used, 1)

            quarters = Quarters(experts)

            def gla(t):
                key = ("gla", t)
                seen(key, "xn")
                for i in range(2):
                    transposes(key, f"x{i}", chunks(xn, i))
                got(key, "x1")
                for name in ("q", "k"):
                    project_T(key, name, next_piece(), [c * P for c in range(4)], xT, P)
                for name in ("v0", "v1", "r0", "r1"):
                    w = next_piece()
                    project(key, name, lambda k: xT[:, k, :], lambda k: w[:, k, :], KD, BANK)
                w, bank = next_piece(), open_bank(key, "low")
                for k in range(KD):
                    last = mm(bank[0:GR, 0:P], w[:, k, :], xT[:, k, :], start=k == 0, stop=k == KD - 1)
                close(key, "low", last)
                got(key, "low")
                bank = open_bank(key, "gate")
                for hh in range(GH):
                    last = mm(bank[:, hh * P:(hh + 1) * P], w_g2[:, hh * GDK:(hh + 1) * GDK], g_low[0:GR, :], start=True, stop=True)
                close(key, "gate", last)
                seen(key, "kd")
                transposes(key, "kd", [g_kd[:, hh, :] for hh in range(GH)])
                bank = open_bank(key, "at")
                for hh in range(GH):
                    for c in range(2):
                        cs = slice(c * CH, (c + 1) * CH)
                        last = mm(bank[cs, hh * CH:(hh + 1) * CH], g_enb[:, hh, cs], g_qT[:, hh, cs], start=True, stop=True)
                close(key, "at", last)
                got(key, "kd")
                for c in range(2):
                    cs = slice(c * CH, (c + 1) * CH)
                    for i in range(2):
                        bank = open_bank(key, f"kv{c}{i}")
                        for e in range(2):
                            hh = 2 * i + e
                            last = mm(bank[:, e * GDV:(e + 1) * GDV], g_kdn[cs, hh, :], g_v[cs, hh * GDV:(hh + 1) * GDV],
                                      start=True, stop=True)
                        close(key, f"kv{c}{i}", last)
                seen(key, "state1")
                for i in range(2):
                    bank = open_bank(key, f"o{i}")
                    for e in range(2):
                        hh = 2 * i + e
                        for c in range(2):
                            cs = slice(c * CH, (c + 1) * CH)
                            dst = bank[cs, e * GDV:(e + 1) * GDV]
                            mm(dst, g_at[cs, hh, :], g_v[cs, hh * GDV:(hh + 1) * GDV], start=True, stop=False)
                            last = mm(dst, g_qT[:, hh, cs], (g_state, g_mid)[c][:, hh, :], start=False, stop=True)
                    close(key, f"o{i}", last)
                seen(key, "on")
                for i in range(2):
                    transposes(key, f"oT{i}", chunks(g_o, i))
                got(key, "oT1")
                for i in range(2):
                    w = next_piece()
                    project(key, f"out{i}", lambda k: xT[:, k, :], lambda k: w[:, k, :], KD, BANK)

            def mix(v):
                key = ("mix", 0)
                for t in range(NT):
                    seen(key, f"xn{t}")
                    for i in range(2):
                        transposes(key, f"x{t}{i}", chunks(x_xn, i))
                got(key, "x11")

                def pair_T(m, x):
                    for i in range(2):
                        w = next_piece()
                        for j in range(2):
                            project_T(key, f"{m}{2 * i + j}", w, [(2 * j + e) * P for e in range(2)], x, S)
                for m in ("cc", "cu", "cb", "q", "k"):
                    pair_T(m, x_xT)
                for i in range(2):
                    w = next_piece()
                    for t in range(NT):
                        project(key, f"v{i}{t}", lambda k: x_xT[:, k, t * P:(t + 1) * P], lambda k: w[:, k, :], KD, BANK)
                w, bank = next_piece(), open_bank(key, "f")
                for k in range(KD):
                    last = mm(bank[0:FH, 0:S], w[:, k, :], x_xT[:, k, :], start=k == 0, stop=k == KD - 1)
                close(key, "f", last)
                for m in ("gc", "ga"):
                    pair_T(m, x_xT)
                seen(key, "cum")
                got(key, "v11")
                for t in range(NT):
                    def score(hh, bank, w):
                        g, half = hh // 2, slice(hh % 2 * FD, (hh % 2 + 1) * FD)
                        qs = slice(t * P, (t + 1) * P)
                        pick = ident[0:FH, hh:hh + 1]
                        mm(bank, x_q[half, g, qs], x_k[half, g, 0:w], start=True, stop=False)
                        mm(bank, x_cum[0:FH, qs], pick.to_broadcast([FH, w]), start=False, stop=False)
                        return mm(bank, pick.to_broadcast([FH, P]), x_ncum[0:FH, 0:w], start=False, stop=True)
                    attend(key, t, score, x_S, x_pT, lambda kt, hh: x_v[:, kt, hh * FD:(hh + 1) * FD])
                seen(key, "convy")
                pair_T("yc", x_cb)
                got(key, "O1_7")
                pair_T("ya", x_oT)
                seen(key, "m")
                for i in range(2):
                    w = next_piece()
                    for t in range(NT):
                        project(key, f"o{i}{t}", lambda k: x_yc[:, k, t * P:(t + 1) * P], lambda k: w[:, k, :], KD, BANK)

            def moe(v):
                key = ("moe", 0)
                for t in range(NT):
                    seen(key, f"xn{t}")
                    for i in range(2):
                        transposes(key, f"x{t}{i}", chunks(hn[:, t, :], i))
                got(key, "x11")
                w = next_piece()
                for t in range(NT):
                    x = e_X[:, t, :].rearrange("p (k n) -> p k n", k=KD)
                    project(key, f"r{t}", lambda k: x[:, k, :], lambda k: w[:, k, :], KD, NG + NE)
                for q in range(6):
                    pe.sem_inc(e_w_used[q], 1)
                seen(key, "picked")
                bank = open_bank(key, "rank")
                mm(bank[:, 0:NE], before[:], e_A[:, 0, :], start=True, stop=True)
                mm(bank[:, NE:2 * NE], ones[:], e_A[:, 0, :], start=True, stop=False)
                mm(bank[:, NE:2 * NE], before[:], e_A[:, 1, :], start=False, stop=True)
                mm(bank[:, 2 * NE:3 * NE], ones[:], e_A[:, 0, :], start=True, stop=False)
                close(key, "rank", mm(bank[:, 2 * NE:3 * NE], ones[:], e_A[:, 1, :], start=False, stop=True))
                got(key, "rank")
                for b in range(4):
                    mm(psum[:, b, :], zeros[:], hn[:, 0, 0:BANK], start=True, stop=False, skip_group_check=True)
                def pair(r, i):
                    n = r * PAIRS + i
                    pe.wait_ge(e_P_ready, n + 1)
                    pe.wait_ge(e_act_ready, 2 * n + 1)
                    for q in range(2):
                        for c in range(4):
                            for t in range(NT):
                                ch = 4 * q + c
                                last = mm(psum[:, 4 + q, c * P:(c + 1) * P], hn[:, t, ch * P:(ch + 1) * P], e_P[:, t, :],
                                          start=t == 0, stop=t == NT - 1)
                        last.then_inc(e_X_filled, 1)
                    pe.wait_ge(e_X_read, 3 * n + 4)
                    for t in range(NT):
                        last = tp(psum[:, 4, t * P:(t + 1) * P], e_Pw[:, t, :], ident[:])
                    last.then_inc(e_X_filled, 1)
                    for e in range(2):
                        rows_T = e_xT[:, :, e * SLOTS:(e + 1) * SLOTS]
                        pe.wait_ge(e_X_read, 3 * n + 5 + e)
                        for m in range(2):
                            w = e_slot(3 * e + m)
                            pe.wait_ge(e_w[3 * e + m], 16 * (n + 1))
                            for j in range(F // P):
                                at = (4 * m + j) * SLOTS
                                for k in range(KD):
                                    last = mm(psum[:, 5 - e, at:at + SLOTS], w[:, k, j * P:(j + 1) * P], rows_T[:, k, :],
                                              start=k == 0, stop=k == KD - 1)
                            if m == 0:
                                last.then_inc(e_w_used[3 * e], 1)
                        last.then_inc(e_gu_filled, 1)
                    for c in range(2):
                        pe.wait_ge(e_y_read, 2 * n + c + 1)
                        for e in range(2):
                            if c == 0:
                                pe.wait_ge(e_act_ready, 2 * n + e + 2)
                                pe.sem_inc(e_w_used[3 * e + 1], 1)
                                pe.wait_ge(e_w[3 * e + 2], 16 * (n + 1))
                            w = e_slot(3 * e + 2)
                            for j in range(F // P):
                                last = mm(psum[e * SLOTS:(e + 1) * SLOTS, 6 + c, :], e_act[:, e, j, :], w[:, j, c * BANK:(c + 1) * BANK],
                                          start=j == 0, stop=j == F // P - 1)
                        last.then_inc(e_y_filled, 1)
                    for c in range(2):
                        pe.wait_ge(e_y_read, 2 * n + c + 3)
                        if c == 1:
                            pe.sem_inc(e_w_used[2], 1)
                            pe.sem_inc(e_w_used[5], 1)
                        for t in range(NT):
                            mm(psum[:, 2 * t + c, :], e_PwT[:, t, :], e_y[:, c * BANK:(c + 1) * BANK],
                               start=False, stop=False, skip_group_check=True)

                pe.wait_ge(act_link, 1)
                pe.sem_inc(e_y_read, 2)
                with pe.Fori(0, PAIRS) as i:
                    pair(0, i)
                most = pe.value_load(e_cnt_i[0:1, 0:1], min_val=0, max_val=S)
                for r in range(1, ROUNDS):
                    with pe.If(most > r * SLOTS):
                        with pe.Fori(0, PAIRS) as i:
                            pair(r, i)
                for b in range(4):
                    last = mm(psum[:, b, :], zeros[:], hn[:, 0, 0:BANK], start=False, stop=True, skip_group_check=True)
                last.then_inc(e_done, 1)

            pe.sem_inc(v_used, RV)
            pe.wait_ge(loaded, 16 * SMALL_LOADS)
            pe.wait_ge(const_ready, 4)
            run = {"mla": mla, "route": route, "gla": gla, "mix": mix, "moe": moe}
            for stage, v in BEFORE:
                run[stage](v)
            for g, beside in enumerate(BESIDE):
                quarters.open(g)
                for stage, v in beside:
                    run[stage](v)
                quarters.close()
            for stage, v in AFTER:
                run[stage](v)
            assert done_jobs == list(JOB), [x for x in zip(done_jobs, JOB) if x[0] != x[1]][:2]


def kernel(**inputs):
    import numpy as _np
    import concourse.bacc as _bacc
    from concourse import mybir as _mybir
    from concourse.bass_utils import run_bass_kernel_spmd as _run

    x = {k: _np.asarray(v) for k, v in inputs.items()}

    def cols(v, k):
        return v.reshape(k, 128).T

    given = {
        "x": x["x"][0], "positions": x["positions"].reshape(2, 128).T,
        "attn_norm_g": x["attn_norm_g"], "ffn_norm_g": x["ffn_norm_g"],
        "mla_w_down": x["mla_w_down"][0], "mla_g_q_lat": x["mla_g_q_lat"], "mla_w_uq": x["mla_w_uq"][0],
        "mla_g_kv_lat": x["mla_g_kv_lat"], "mla_w_ukv": x["mla_w_ukv"][0], "mla_g_qn": x["mla_g_qn"],
        "mla_g_kn": x["mla_g_kn"], "mla_w_o": x["mla_w_o"][0], "gla_w_in": x["gla_w_in"][0],
        "gla_w_g2": x["gla_w_g2"][0], "gla_b_g": cols(x["gla_b_g"][0], 4), "gla_g_on": x["gla_g_on"],
        "gla_w_o": x["gla_w_o"][0], "peer_w_query": x["peer_w_query"],
        "sub_keys": x["peer_sub_keys"].transpose(1, 3, 0, 2).reshape(128, 2, 128),
        "peer_u0": x["peer_u"][0], "peer_u1": x["peer_u"][1], "peer_v0": x["peer_v"][0], "peer_v1": x["peer_v"][1],
        "norm_mix_g_2": x["norm_mix_g_2"][None], "w_in_2": x["w_in_2"],
        "conv_w_2": x["conv_w_2"].reshape(3, 8, 128).transpose(2, 0, 1), "conv_b_2": cols(x["conv_b_2"], 8),
        "b_forget_2": x["b_forget_2"][:, None], "w_conv_out_2": x["w_conv_out_2"], "w_att_out_2": x["w_att_out_2"],
        "w_out_2": x["w_out_2"], "norm_ffn_g_2": x["norm_ffn_g_2"][None],
        "w_router": _np.concatenate([x["w_router_group_2"], x["w_router_expert_2"].transpose(1, 0, 2).reshape(1024, 32)], 1),
        "w_e_gate_2": x["w_e_gate_2"], "w_e_up_2": x["w_e_up_2"], "w_e_down_2": x["w_e_down_2"],
        "norm_final_g_2": x["norm_final_g_2"][None],
    }
    nc = _bacc.Bacc("TRN2", target_bir_lowering=False, num_devices=1)
    arrays, a = {}, {}
    for name, v in given.items():
        v = _np.ascontiguousarray(v)
        arrays[f"in_{name}"] = v
        a[name] = nc.dram_tensor(f"in_{name}", v.shape, _mybir.dt.from_np(v.dtype), kind="ExternalInput").ap()
    a["peer_u"], a["peer_v"] = [a["peer_u0"], a["peer_u1"]], [a["peer_v0"], a["peer_v1"]]
    out = nc.dram_tensor("out_0", (256, 1024), _mybir.dt.float32, kind="ExternalOutput").ap()
    build(nc, a, out)
    r = _run(nc, [arrays], core_ids=[0])
    return r.results[0]["out_0"].reshape(1, 256, 1024)
```
